# Optimizing a Trainium2 kernel written in Bass

```python
import math
import jax, jax.numpy as jnp
from jax import lax
import numpy as np

D_MODEL = 1024
BATCH = 1
SEQ = 2048
DEPTH = 1

N_MIXERS = 3
LN_EPS = 1e-5
NORM_EPS = 1e-6
CONV_K = 4
GDN_HEADS = 8
GDN_DK = 128
GDN_DV = 128
GDN_QK = GDN_HEADS * GDN_DK
GDN_V = GDN_HEADS * GDN_DV
GDN_CHUNK = 64
LRU_WIDTH = D_MODEL
LRU_BLOCKS = 16
LRU_BW = LRU_WIDTH // LRU_BLOCKS
RG_C = 8.0
NSA_HEADS = 16
NSA_GROUPS = 4
NSA_HPG = NSA_HEADS // NSA_GROUPS
NSA_DK = 64
NSA_Q = NSA_HEADS * NSA_DK
NSA_KV = NSA_GROUPS * NSA_DK
CMP_LEN = 32
CMP_STRIDE = 16
CMP_HID = 256
SLC_LEN = 64
N_SEL = 16
WINDOW = 512
Q_BLOCK = 128
N_GROUPS = 4
EXP_PER_GROUP = 8
N_EXPERTS = N_GROUPS * EXP_PER_GROUP
TOP_K = 2
D_EXPERT = 512
EXPERT_BLOCK = 256
NEG = -1e30
BIG = 1e30

kernel_name = 'hybrid_gdn_rglru_nsa_hmoe_trunk'

def layer_norm(x, g, b):
    xf = x.astype(jnp.float32)
    mu = jnp.mean(xf, -1, keepdims=True)
    xc = xf - mu
    var = jnp.mean(xc * xc, -1, keepdims=True)
    return (xc * lax.rsqrt(var + LN_EPS) * g + b).astype(x.dtype)

def causal_dwconv(x, w):
    k = w.shape[0]
    return lax.conv_general_dilated(x, w[:, None, :].astype(x.dtype), window_strides=(1,), padding=[(k - 1, 0)],
                                    dimension_numbers=('NWC', 'WIO', 'NWC'), feature_group_count=x.shape[-1])

def l2_normalize(x):
    xf = x.astype(jnp.float32)
    return xf * lax.rsqrt(jnp.sum(xf * xf, -1, keepdims=True) + NORM_EPS)

def masked_softmax(s, mask):
    s = jnp.where(mask, s.astype(jnp.float32), NEG)
    return jax.nn.softmax(s, axis=-1) * mask

def chunk_gated_delta_rule(q, k, v, g, beta):
    B, T, H, DK = q.shape
    DV = v.shape[-1]
    C = GDN_CHUNK
    N = T // C

    def chunks(t):
        return jnp.moveaxis(t.reshape((B, N, C, H) + t.shape[3:]), 3, 1)

    q = chunks(q) * (DK ** -0.5)
    k = chunks(k)
    v = chunks(v)
    gc = jnp.cumsum(chunks(g), axis=-1)
    bt = chunks(beta)[..., None]
    kb = k * bt
    vb = v * bt
    ii = jnp.arange(C)
    causal = ii[:, None] >= ii[None, :]
    strict = ii[:, None] > ii[None, :]
    decay = jnp.exp(jnp.where(causal, gc[..., :, None] - gc[..., None, :], -jnp.inf))
    lmat = jnp.einsum('bhnid,bhnjd->bhnij', kb, k) * decay * strict
    amat = lmat + jnp.eye(C, dtype=jnp.float32)
    u = lax.linalg.triangular_solve(amat, vb, left_side=True, lower=True, unit_diagonal=True)
    w = lax.linalg.triangular_solve(amat, kb * jnp.exp(gc)[..., None], left_side=True, lower=True, unit_diagonal=True)
    qk = jnp.einsum('bhnid,bhnjd->bhnij', q, k) * decay

    def step(S, xs):
        qn, kn, un, wn, gn, qkn = xs
        v_new = un - jnp.einsum('bhck,bhkv->bhcv', wn, S)
        o = (jnp.einsum('bhck,bhkv->bhcv', qn * jnp.exp(gn)[..., None], S)
             + jnp.einsum('bhij,bhjv->bhiv', qkn, v_new))
        g_last = gn[..., -1:]
        S = (S * jnp.exp(g_last)[..., None]
             + jnp.einsum('bhck,bhcv->bhkv', kn * jnp.exp(g_last - gn)[..., None], v_new))
        return S, o

    xs = tuple(jnp.moveaxis(t, 2, 0) for t in (q, k, u, w, gc, qk))
    S0 = jnp.zeros((B, H, DK, DV), jnp.float32)
    _, o = lax.scan(step, S0, xs)
    return jnp.moveaxis(o, 0, 2).transpose(0, 2, 3, 1, 4).reshape(B, T, H, DV)

def gdn_mixer(h, w_in, conv_w, a_log, dt_bias, norm_g, w_out):
    B, T, _ = h.shape
    p = h @ w_in
    s0 = 2 * GDN_QK + GDN_V
    qkv, z, a, b = jnp.split(p, [s0, s0 + GDN_V, s0 + GDN_V + GDN_HEADS], axis=-1)
    qkv = jax.nn.silu(causal_dwconv(qkv, conv_w))
    q, k, v = jnp.split(qkv, [GDN_QK, 2 * GDN_QK], axis=-1)
    q = l2_normalize(q.reshape(B, T, GDN_HEADS, GDN_DK))
    k = l2_normalize(k.reshape(B, T, GDN_HEADS, GDN_DK))
    v = v.reshape(B, T, GDN_HEADS, GDN_DV).astype(jnp.float32)
    beta = jax.nn.sigmoid(b.astype(jnp.float32))
    g = -jnp.exp(a_log.astype(jnp.float32)) * jax.nn.softplus(a.astype(jnp.float32) + dt_bias.astype(jnp.float32))
    o = chunk_gated_delta_rule(q, k, v, g, beta)
    o = o * lax.rsqrt(jnp.mean(o * o, -1, keepdims=True) + NORM_EPS) * norm_g
    o = o * jax.nn.silu(z.reshape(B, T, GDN_HEADS, GDN_DV).astype(jnp.float32))
    return o.reshape(B, T, GDN_V).astype(h.dtype) @ w_out

def _lin_rec_combine(left, right):
    a1, b1 = left
    a2, b2 = right
    return a1 * a2, a2 * b1 + b2

def rglru_mixer(h, w_in, conv_w, conv_b, w_a, b_a, w_x, b_x, lam, w_out):
    B, T, _ = h.shape
    gate_br, xb = jnp.split(h @ w_in, [LRU_WIDTH], axis=-1)
    xb = causal_dwconv(xb, conv_w) + conv_b
    xh = xb.reshape(B, T, LRU_BLOCKS, LRU_BW)
    r = jax.nn.sigmoid((jnp.einsum('btni,nij->btnj', xh, w_a).reshape(B, T, LRU_WIDTH) + b_a).astype(jnp.float32))
    i_g = jax.nn.sigmoid((jnp.einsum('btni,nij->btnj', xh, w_x).reshape(B, T, LRU_WIDTH) + b_x).astype(jnp.float32))
    log_a = -RG_C * r * jax.nn.softplus(-lam.astype(jnp.float32))
    a = jnp.exp(log_a)
    mult = jnp.sqrt(jnp.maximum(-jnp.expm1(2.0 * log_a), 0.0))
    u = mult * i_g * xb.astype(jnp.float32)
    _, hs = lax.associative_scan(_lin_rec_combine, (a, u), axis=1)
    y = hs * jax.nn.gelu(gate_br.astype(jnp.float32))
    return y.astype(h.dtype) @ w_out

def nsa_mixer(h, w_in, pe_k, pe_v, ck_w1, ck_w2, cv_w1, cv_w2, w_out):
    B, T, _ = h.shape
    G, P, DK = NSA_GROUPS, NSA_HPG, NSA_DK
    scale = DK ** -0.5
    cuts = [NSA_Q + j * NSA_KV for j in range(7)]
    q, kc, vc, ks, vs, kw, vw, gates = jnp.split(h @ w_in, cuts, axis=-1)
    q = q.reshape(B, T, G, P, DK)
    kc, vc, ks, vs, kw, vw = [t.reshape(B, T, G, DK) for t in (kc, vc, ks, vs, kw, vw)]
    gates = jax.nn.sigmoid(gates.astype(jnp.float32)).reshape(B, T, G, P, 3)

    n_cmp = (T - CMP_LEN) // CMP_STRIDE + 1
    cidx = jnp.arange(n_cmp)[:, None] * CMP_STRIDE + jnp.arange(CMP_LEN)[None, :]

    def compress(t, pe, w1, w2):
        blk = t[:, cidx] + pe[None, None, :, None, :]
        flat = blk.transpose(0, 1, 3, 2, 4).reshape(B, n_cmp, G, CMP_LEN * DK)
        return jax.nn.gelu(flat @ w1) @ w2

    kcmp = compress(kc, pe_k, ck_w1, ck_w2)
    vcmp = compress(vc, pe_v, cv_w1, cv_w2)
    cmp_end = jnp.arange(n_cmp) * CMP_STRIDE + CMP_LEN - 1

    n_slc = T // SLC_LEN
    n_sel = min(N_SEL, n_slc)
    ci = jnp.arange(n_cmp)[:, None] * CMP_STRIDE
    sj = jnp.arange(n_slc)[None, :] * SLC_LEN
    overlap = jnp.clip(jnp.minimum(ci + CMP_LEN, sj + SLC_LEN) - jnp.maximum(ci, sj), 0, None).astype(jnp.float32) / CMP_LEN
    ks_t = ks.reshape(B, n_slc, SLC_LEN, G, DK).transpose(0, 3, 1, 2, 4)
    vs_t = vs.reshape(B, n_slc, SLC_LEN, G, DK).transpose(0, 3, 1, 2, 4)
    b_ix = jnp.arange(B)[:, None, None, None]
    g_ix = jnp.arange(G)[None, :, None, None]
    s_idx = jnp.arange(n_slc)[None, :]

    kw_pad = jnp.pad(kw, ((0, 0), (WINDOW, 0), (0, 0), (0, 0)))
    vw_pad = jnp.pad(vw, ((0, 0), (WINDOW, 0), (0, 0), (0, 0)))

    n_qb = T // Q_BLOCK
    qb = jnp.moveaxis(q.reshape(B, n_qb, Q_BLOCK, G, P, DK), 1, 0)
    gb = jnp.moveaxis(gates.reshape(B, n_qb, Q_BLOCK, G, P, 3), 1, 0)

    def block(args):
        qi, gi, bidx = args
        t0 = bidx * Q_BLOCK
        tpos = t0 + jnp.arange(Q_BLOCK)
        s_c = jnp.einsum('bqgpd,bngd->bgpqn', qi, kcmp) * scale
        p_c = masked_softmax(s_c, cmp_end[None, :] <= tpos[:, None])
        o_c = jnp.einsum('bgpqn,bngd->bqgpd', p_c, vcmp)
        imp = jnp.einsum('bgpqn,ns->bgqs', p_c, overlap)
        cur = (tpos // SLC_LEN)[:, None]
        forced = (s_idx == 0) | (s_idx == cur) | (s_idx == cur - 1)
        imp = jnp.where(forced, BIG, imp)
        imp = jnp.where(sj <= tpos[:, None], imp, -BIG)
        _, sel = lax.top_k(imp, n_sel)
        kg = ks_t[b_ix, g_ix, sel]
        vg = vs_t[b_ix, g_ix, sel]
        kpos = (sel[..., None] * SLC_LEN + jnp.arange(SLC_LEN)).reshape(B, G, Q_BLOCK, n_sel * SLC_LEN)
        s_s = jnp.einsum('bqgpd,bgqnld->bgpqnl', qi, kg).reshape(B, G, P, Q_BLOCK, n_sel * SLC_LEN) * scale
        p_s = masked_softmax(s_s, (kpos <= tpos[None, None, :, None])[:, :, None])
        o_s = jnp.einsum('bgpqm,bgqmd->bqgpd', p_s, vg.reshape(B, G, Q_BLOCK, n_sel * SLC_LEN, DK))
        kwin = lax.dynamic_slice_in_dim(kw_pad, t0, Q_BLOCK + WINDOW, axis=1)
        vwin = lax.dynamic_slice_in_dim(vw_pad, t0, Q_BLOCK + WINDOW, axis=1)
        kpos_w = t0 - WINDOW + jnp.arange(Q_BLOCK + WINDOW)
        mask_w = ((kpos_w[None, :] <= tpos[:, None]) & (kpos_w[None, :] > tpos[:, None] - WINDOW)
                  & (kpos_w[None, :] >= 0))
        s_w = jnp.einsum('bqgpd,bkgd->bgpqk', qi, kwin) * scale
        p_w = masked_softmax(s_w, mask_w)
        o_w = jnp.einsum('bgpqk,bkgd->bqgpd', p_w, vwin)
        return gi[..., 0:1] * o_c + gi[..., 1:2] * o_s + gi[..., 2:3] * o_w

    ob = lax.map(block, (qb, gb, jnp.arange(n_qb)))
    o = jnp.moveaxis(ob, 0, 1).reshape(B, T, NSA_Q)
    return o.astype(h.dtype) @ w_out

def expert_dispatch(xf, expert_idx, gate, w_gate, w_up, w_down):
    N, D = xf.shape
    K = expert_idx.shape[1]
    E = w_gate.shape[0]
    A = N * K
    flat_e = expert_idx.reshape(-1).astype(jnp.int32)
    order = jnp.argsort(flat_e).astype(jnp.int32)
    sorted_e = flat_e[order]
    tok = order // K
    counts = jnp.bincount(flat_e, length=E)
    padded = (counts + EXPERT_BLOCK - 1) // EXPERT_BLOCK * EXPERT_BLOCK
    pad_end = jnp.cumsum(padded)
    pad_start = pad_end - padded
    start = jnp.cumsum(counts) - counts
    dest = pad_start[sorted_e] + jnp.arange(A, dtype=jnp.int32) - start[sorted_e]
    n_blk = -(-A // EXPERT_BLOCK) + E
    rows = n_blk * EXPERT_BLOCK
    src = jnp.full((rows,), N, jnp.int32).at[dest].set(tok)
    blk_e = jnp.minimum(jnp.searchsorted(pad_end, jnp.arange(n_blk) * EXPERT_BLOCK, side='right'), E - 1)
    xpad = jnp.concatenate([xf, jnp.zeros((1, D), xf.dtype)], axis=0)
    xb = xpad[src].reshape(n_blk, EXPERT_BLOCK, D)

    def ffn(args):
        xi, e = args
        return (jax.nn.silu(xi @ w_gate[e]) * (xi @ w_up[e])) @ w_down[e]

    yb = lax.map(ffn, (xb, blk_e)).reshape(rows, D)
    contrib = yb[dest] * gate.reshape(-1)[order][:, None].astype(yb.dtype)
    return jnp.zeros((N, D), yb.dtype).at[tok].add(contrib)

def hier_moe(h, w_grp, b_grp, w_exp, b_exp, w_gate, w_up, w_down):
    B, T, D = h.shape
    xf = h.reshape(B * T, D)
    n = xf.shape[0]
    grp_p = jax.nn.softmax((xf @ w_grp + b_grp).astype(jnp.float32), axis=-1)
    gp, gi = lax.top_k(grp_p, 1)
    exp_logits = (xf @ w_exp + b_exp).astype(jnp.float32).reshape(n, N_GROUPS, EXP_PER_GROUP)
    in_grp = exp_logits[jnp.arange(n), gi[:, 0]]
    wv, wi = lax.top_k(jax.nn.softmax(in_grp, axis=-1), TOP_K)
    wv = wv / jnp.sum(wv, -1, keepdims=True)
    gate = gp * wv
    expert_idx = gi * EXP_PER_GROUP + wi
    return expert_dispatch(xf, expert_idx, gate, w_gate, w_up, w_down).reshape(B, T, D)

def setup_inputs(seed: int = 0) -> dict:
    key = jax.random.key(seed)
    ks = iter(jax.random.split(key, 64))
    f32 = jnp.float32
    D = D_MODEL
    beta = (8.0 * DEPTH) ** -0.25
    n_a = len(range(0, DEPTH, N_MIXERS))
    n_b = len(range(1, DEPTH, N_MIXERS))
    n_c = len(range(2, DEPTH, N_MIXERS))

    def nrm(shape, s):
        return jax.random.normal(next(ks), shape, f32) * s

    def unif(shape, lo, hi):
        return jax.random.uniform(next(ks), shape, f32, lo, hi)

    dt = jnp.exp(unif((n_a, GDN_HEADS), math.log(1e-3), math.log(1e-1)))
    a0 = unif((n_b, LRU_WIDTH), 0.9, 0.999) ** (1.0 / RG_C)
    gdn_cols = 2 * GDN_QK + 2 * GDN_V + 2 * GDN_HEADS
    nsa_cols = NSA_Q + 6 * NSA_KV + 3 * NSA_HEADS
    return {
        'x': nrm((BATCH, SEQ, D), 1.0),
        'c': nrm((BATCH, D), 1.0),
        'ada_w': nrm((DEPTH, D, 6 * D), 0.1 * D ** -0.5),
        'ada_b': nrm((DEPTH, 6 * D), 0.01),
        'ln1_g': 1.0 + nrm((DEPTH, D), 0.02),
        'ln1_b': nrm((DEPTH, D), 0.02),
        'ln2_g': 1.0 + nrm((DEPTH, D), 0.02),
        'ln2_b': nrm((DEPTH, D), 0.02),
        'gdn_w_in': nrm((n_a, D, gdn_cols), D ** -0.5),
        'gdn_conv_w': nrm((n_a, CONV_K, 2 * GDN_QK + GDN_V), CONV_K ** -0.5),
        'gdn_a_log': jnp.log(unif((n_a, GDN_HEADS), 1.0, 16.0)),
        'gdn_dt_bias': dt + jnp.log(-jnp.expm1(-dt)),
        'gdn_norm_g': 1.0 + nrm((n_a, GDN_DV), 0.02),
        'gdn_w_out': nrm((n_a, GDN_V, D), GDN_V ** -0.5 * beta),
        'lru_w_in': nrm((n_b, D, 2 * LRU_WIDTH), D ** -0.5),
        'lru_conv_w': nrm((n_b, CONV_K, LRU_WIDTH), CONV_K ** -0.5),
        'lru_conv_b': nrm((n_b, LRU_WIDTH), 0.01),
        'lru_w_a': nrm((n_b, LRU_BLOCKS, LRU_BW, LRU_BW), LRU_BW ** -0.5),
        'lru_b_a': nrm((n_b, LRU_WIDTH), 0.01),
        'lru_w_x': nrm((n_b, LRU_BLOCKS, LRU_BW, LRU_BW), LRU_BW ** -0.5),
        'lru_b_x': nrm((n_b, LRU_WIDTH), 0.01),
        'lru_lambda': jnp.log(a0) - jnp.log1p(-a0),
        'lru_w_out': nrm((n_b, LRU_WIDTH, D), LRU_WIDTH ** -0.5 * beta),
        'nsa_w_in': nrm((n_c, D, nsa_cols), D ** -0.5),
        'nsa_pe_k': nrm((n_c, CMP_LEN, NSA_DK), 0.02),
        'nsa_pe_v': nrm((n_c, CMP_LEN, NSA_DK), 0.02),
        'nsa_ck_w1': nrm((n_c, CMP_LEN * NSA_DK, CMP_HID), (CMP_LEN * NSA_DK) ** -0.5),
        'nsa_ck_w2': nrm((n_c, CMP_HID, NSA_DK), CMP_HID ** -0.5),
        'nsa_cv_w1': nrm((n_c, CMP_LEN * NSA_DK, CMP_HID), (CMP_LEN * NSA_DK) ** -0.5),
        'nsa_cv_w2': nrm((n_c, CMP_HID, NSA_DK), CMP_HID ** -0.5),
        'nsa_w_out': nrm((n_c, NSA_Q, D), NSA_Q ** -0.5 * beta),
        'moe_w_grp': nrm((DEPTH, D, N_GROUPS), D ** -0.5),
        'moe_b_grp': nrm((DEPTH, N_GROUPS), 0.01),
        'moe_w_exp': nrm((DEPTH, D, N_EXPERTS), D ** -0.5),
        'moe_b_exp': nrm((DEPTH, N_EXPERTS), 0.01),
        'moe_w_gate': nrm((DEPTH, N_EXPERTS, D, D_EXPERT), D ** -0.5),
        'moe_w_up': nrm((DEPTH, N_EXPERTS, D, D_EXPERT), D ** -0.5),
        'moe_w_down': nrm((DEPTH, N_EXPERTS, D_EXPERT, D), D_EXPERT ** -0.5 * beta),
    }

def reference(x, c, ada_w, ada_b, ln1_g, ln1_b, ln2_g, ln2_b,
              gdn_w_in, gdn_conv_w, gdn_a_log, gdn_dt_bias, gdn_norm_g, gdn_w_out,
              lru_w_in, lru_conv_w, lru_conv_b, lru_w_a, lru_b_a, lru_w_x, lru_b_x, lru_lambda, lru_w_out,
              nsa_w_in, nsa_pe_k, nsa_pe_v, nsa_ck_w1, nsa_ck_w2, nsa_cv_w1, nsa_cv_w2, nsa_w_out,
              moe_w_grp, moe_b_grp, moe_w_exp, moe_b_exp, moe_w_gate, moe_w_up, moe_w_down):
    alpha = (2.0 * DEPTH) ** 0.25
    cond = jax.nn.silu(c)
    ja = jb = jc = 0
    for i in range(DEPTH):
        mod = (cond @ ada_w[i] + ada_b[i])[:, None, :]
        sh1, sc1, gt1, sh2, sc2, gt2 = jnp.split(mod, 6, axis=-1)
        hm = x * (1.0 + sc1) + sh1
        kind = i % N_MIXERS
        if kind == 0:
            y = gdn_mixer(hm, gdn_w_in[ja], gdn_conv_w[ja], gdn_a_log[ja], gdn_dt_bias[ja], gdn_norm_g[ja], gdn_w_out[ja])
            ja += 1
        elif kind == 1:
            y = rglru_mixer(hm, lru_w_in[jb], lru_conv_w[jb], lru_conv_b[jb], lru_w_a[jb], lru_b_a[jb],
                            lru_w_x[jb], lru_b_x[jb], lru_lambda[jb], lru_w_out[jb])
            jb += 1
        else:
            y = nsa_mixer(hm, nsa_w_in[jc], nsa_pe_k[jc], nsa_pe_v[jc], nsa_ck_w1[jc], nsa_ck_w2[jc],
                          nsa_cv_w1[jc], nsa_cv_w2[jc], nsa_w_out[jc])
            jc += 1
        x = layer_norm(alpha * x + (1.0 + gt1) * y, ln1_g[i], ln1_b[i])
        hf = x * (1.0 + sc2) + sh2
        y = hier_moe(hf, moe_w_grp[i], moe_b_grp[i], moe_w_exp[i], moe_b_exp[i],
                     moe_w_gate[i], moe_w_up[i], moe_w_down[i])
        x = layer_norm(alpha * x + (1.0 + gt2) * y, ln2_g[i], ln2_b[i])
    return x


_drawn_inputs = setup_inputs


def setup_inputs(seed=0):
    import zlib

    import numpy as np

    out = dict(_drawn_inputs(seed))
    spreads = {}
    factors = {'ada_b': 3.401,
     'ln2_g': 8.958,
     'ln2_b': 8.547,
     'gdn_norm_g': 5.295,
     'moe_b_grp': 44.327,
     'moe_b_exp': 18.19}
    for name, (base, spread) in spreads.items():
        noise = np.random.default_rng([zlib.crc32(name.encode()), seed]).standard_normal(out[name].shape)
        drawn = base * np.exp(spread * noise) if base else spread * noise
        out[name] = __import__('jax').numpy.asarray(drawn.astype(out[name].dtype))
    for name, factor in factors.items():
        out[name] = (out[name] * factor).astype(out[name].dtype)
    return out
```

```python
import concourse.bass as bass
from concourse import mybir
from contextlib import ExitStack

F32 = mybir.dt.float32
F32R = mybir.dt.float32r
I32 = mybir.dt.int32
U32 = mybir.dt.uint32
ALU = mybir.AluOpType
ACT = mybir.ActivationFunctionType
AX = mybir.AxisListType

P = 128
D = 1024
SEQ = 2048
KT = D // P
H = 8
NT = SEQ // P
QT = 4
QW = QT * P
NQ = NT // QT
ITEMS = NQ * H
G, EPG = 4, 8
E = G * EPG
DE = 512
FT = DE // P
TAPS = 4
NSC = 7


def allocators(nc, ctx, phase):
    sems = []
    ctx.callback(nc.all_engine_barrier)
    ctx.callback(lambda: nc.clear_and_free_semaphores(sems))

    def sb(name, shape, dtype=F32):
        return ctx.enter_context(nc.sbuf_tensor(f"{phase}_{name}", shape, dtype))

    def ps(name, shape, dtype=F32):
        return ctx.enter_context(nc.psum_tensor(f"{phase}_{name}", shape, dtype))

    def sem(name):
        sems.append(nc.alloc_semaphore(f"{phase}_{name}"))
        return sems[-1]

    return sb, ps, sem



def conditioning_phase(nc, c, x, ada_w, ada_b, w_in, a_log, dt_bias, mod_rows, hm_split, gate_scalars):
    with ExitStack() as ctx:
        sb, ps, sem = allocators(nc, ctx, "cond")
        cond = sb("cond", [P, KT])
        cond_tanh = sb("cond_tanh", [P, KT])
        ada = [sb(f"ada{i}", [P, KT, D]) for i in range(2)]
        bias_row = sb("bias_row", [1, 6 * D])
        mod_row = sb("mod_row", [1, 6 * D])
        scale_col = sb("scale_col", [P, KT])
        shift_col = sb("shift_col", [P, KT])
        x_tok = sb("x_tok", [P, QT, D])
        hm_f = sb("hm_f", [P, 2, QW])
        hm = sb("hm", [P, 2, KT, QW], F32R)
        wab = sb("wab", [P, KT, 2 * H])
        wab_hi = sb("wab_hi", [P, KT, 2 * H], F32R)
        wab_lo = sb("wab_lo", [P, KT, 2 * H], F32R)
        ident = sb("ident", [P, P])
        ab = sb("ab", [P, NT, 2 * H])
        upper = sb("upper", [P, P])
        ones = sb("ones", [P, P])
        dt_row = sb("dt_row", [P, H])
        al_row = sb("al_row", [P, H])
        work = sb("work", [P, 8, NT, H])
        out_sc = sb("out_sc", [P, NQ, H, NSC, QT])
        p_mod = ps("p_mod", [1, 2, QW])
        p_x = ps("p_x", [P, 2, QW])
        p_ab = ps("p_ab", [P, 2, QW])
        p_cum = ps("p_cum", [P, QW])
        p_tot = ps("p_tot", [P, QW])

        c_loaded, small_loaded, wab_loaded, x_loaded, mod_stored, cols_loaded, hm_stored, sc_stored = (
            sem(n) for n in "c_loaded small_loaded wab_loaded x_loaded mod_stored cols_loaded hm_stored sc_stored".split())
        ada_loaded = [sem("ada_loaded0"), sem("ada_loaded1")]
        (cond_ready, cond_tanh_ready, ident_ready, part_done, part_added, part_fixed, x_transposed, x_mod, hm_hi, hm_lo,
         wab_hi_ready, wab_lo_ready, ab_done, ab_saved, chain, chain_act, cum_done, const_ready) = (
            sem(n) for n in ("cond_ready cond_tanh_ready ident_ready part_done part_added part_fixed x_transposed x_mod "
                             "hm_hi hm_lo wab_hi_ready wab_lo_ready ab_done ab_saved chain chain_act cum_done "
                             "const_ready").split())
        w_in_v = w_in.rearrange("(k p) n -> p k n", p=P)
        ada_v = ada_w.rearrange("(k p) n -> p k n", p=P)
        x_v = x.rearrange("(q t p) d -> q p t d", p=P, t=QT)
        block = ctx.enter_context(nc.Block())

        @block.sync
        def _(sp):
            with nc.allow_non_contiguous_dma(reason="one value on each partition"):
                sp.dma_start(cond[:], c.rearrange("b (k p) -> p (b k)", p=P)).then_inc(c_loaded, 16)
            for j in range(2):
                sp.dma_start(ada[j][:], ada_v[:, :, j * D:(j + 1) * D]).then_inc(ada_loaded[j], 16)
                if j == 0:
                    sp.dma_start(bias_row[:], ada_b).then_inc(small_loaded, 16)
                    sp.dma_start(dt_row[:], dt_bias.to_broadcast([P, H])).then_inc(small_loaded, 16)
                    sp.dma_start(al_row[:], a_log.to_broadcast([P, H])).then_inc(small_loaded, 16)
            sp.dma_start(wab[:], w_in_v[:, :, 4 * D:4 * D + 2 * H]).then_inc(wab_loaded, 16)
            sp.dma_start(x_tok[:], x_v[0]).then_inc(x_loaded, 16)
            for j in range(2, 4):
                sp.wait_ge(part_done, j - 1)
                sp.dma_start(ada[j % 2][:], ada_v[:, :, j * D:(j + 1) * D]).then_inc(ada_loaded[j % 2], 16)
            sp.wait_ge(part_added, 2)
            sp.wait_ge(part_fixed, 1)
            sp.dma_start(mod_rows[0:1, 0:2 * D], mod_row[:, 0:2 * D]).then_inc(mod_stored, 16)
            sp.wait_ge(mod_stored, 16)
            with nc.allow_non_contiguous_dma(reason="one value on each partition"):
                sp.dma_start(shift_col[:], mod_rows[0:1, 0:D].rearrange("b (k p) -> p (b k)", p=P)).then_inc(cols_loaded, 16)
                sp.dma_start(scale_col[:], mod_rows[0:1, D:2 * D].rearrange("b (k p) -> p (b k)", p=P)).then_inc(cols_loaded, 16)
            for q in range(NQ):
                if q < NQ - 1:
                    sp.wait_ge(x_transposed, KT * (q + 1))
                    sp.dma_start(x_tok[:], x_v[q + 1]).then_inc(x_loaded, 16)
                if q < 2:
                    sp.wait_ge(part_done, q + 3)
                    sp.dma_start(ada[q % 2][:], ada_v[:, :, (q + 4) * D:(q + 5) * D]).then_inc(ada_loaded[q % 2], 16)
                sp.wait_ge(hm_hi, KT * (q + 1))
                sp.wait_ge(hm_lo, KT * (q + 1))
                sp.dma_start(hm_split[q], hm[:].bitcast(F32)).then_inc(hm_stored, 16)
            sp.wait_ge(part_fixed, 4)
            sp.wait_ge(part_added, 6)
            sp.dma_start(mod_rows[0:1, 2 * D:], mod_row[:, 2 * D:]).then_inc(mod_stored, 16)
            sp.wait_ge(chain, 100)
            sp.dma_start(gate_scalars, out_sc[:].rearrange("p q h s t -> p (q h s t)")).then_inc(sc_stored, 16)
            sp.wait_ge(sc_stored, 16)
            sp.wait_ge(mod_stored, 32)
            sp.wait_ge(hm_stored, 16 * NQ)

        @block.gpsimd
        def _(pool):
            nc.gpsimd.memset(ident[:], 0.0).then_inc(ident_ready, 1)
            nc.gpsimd.memset(ones[:], 1.0).then_inc(const_ready, 1)
            nc.gpsimd.memset(upper[:], 1.0).then_inc(const_ready, 1)
            pool.wait_ge(ident_ready, 1)
            nc.gpsimd.affine_select(out=ident[:], in_=ident[:], compare_op=ALU.not_equal, fill=1.0, base=0,
                                    pattern=[[-1, P]], channel_multiplier=1).then_inc(ident_ready, 1)
            pool.wait_ge(const_ready, 2)
            nc.gpsimd.affine_select(out=upper[:], in_=upper[:], compare_op=ALU.is_ge, fill=0.0, base=0,
                                    pattern=[[1, P]], channel_multiplier=-1).then_inc(const_ready, 1)

        @block.tensor
        def _(pe):
            def part(j):
                pe.wait_ge(ada_loaded[j % 2], 16 * (j // 2 + 1))
                if j >= 1:
                    pe.wait_ge(part_added, j)
                for n in range(2):
                    for k in range(KT):
                        last = nc.tensor.matmul(p_mod[:, n, :], cond[:, k:k + 1], ada[j % 2][:, k, n * QW:(n + 1) * QW],
                                                start=(k == 0), stop=(k == KT - 1))
                last.then_inc(part_done, 1)

            pe.wait_ge(cond_ready, 1)
            part(0)
            part(1)
            pe.wait_ge(ident_ready, 2)
            pe.wait_ge(wab_hi_ready, 1)
            pe.wait_ge(wab_lo_ready, 1)
            for q in range(NQ):
                pe.wait_ge(x_loaded, 16 * (q + 1))
                for k in range(KT):
                    n = KT * q + k
                    if n >= 2:
                        pe.wait_ge(x_mod, n - 1)
                    for t in range(QT):
                        last = nc.tensor.transpose(p_x[:, n % 2, t * P:(t + 1) * P], x_tok[:, t, k * P:(k + 1) * P], ident[:])
                    last.then_inc(x_transposed, 1)
                part(q + 2)
                pe.wait_ge(hm_hi, KT * (q + 1))
                pe.wait_ge(hm_lo, KT * (q + 1))
                for t in range(QT):
                    n = QT * q + t
                    if n >= 2:
                        pe.wait_ge(ab_saved, n - 1)
                    for k in range(KT):
                        tok = slice(t * P, (t + 1) * P)
                        for s, (a, w) in enumerate(((0, wab_hi), (0, wab_lo), (1, wab_hi))):
                            last = nc.tensor.matmul(p_ab[:, n % 2, 0:2 * H], hm[:, a, k, tok], w[:, k, :],
                                                    start=(k == 0 and s == 0), stop=(k == KT - 1 and s == 2))
                    last.then_inc(ab_done, 1)
            pe.wait_ge(chain, 7)
            pe.wait_ge(const_ready, 3)
            g = work[:, 0].rearrange("p t h -> p (t h)")
            nc.tensor.matmul(p_cum[:, 0:NT * H], upper[:], g, start=True, stop=True).then_inc(cum_done, 1)
            nc.tensor.matmul(p_tot[:, 0:NT * H], ones[:], g, start=True, stop=True).then_inc(cum_done, 1)

        @block.scalar
        def _(act):
            act.wait_ge(c_loaded, 16)
            nc.scalar.activation(cond_tanh[:], cond[:], ACT.Tanh, scale=0.5).then_inc(cond_tanh_ready, 1)
            act.wait_ge(cols_loaded, 32)
            for q in range(NQ):
                for k in range(KT):
                    n = KT * q + k
                    act.wait_ge(x_transposed, n + 1)
                    if n >= 2:
                        act.wait_ge(hm_lo, n - 1)
                    nc.scalar.activation(hm_f[:, n % 2, :], p_x[:, n % 2, :], ACT.Identity,
                                         bias=shift_col[:, k:k + 1], scale=scale_col[:, k:k + 1]).then_inc(x_mod, 1)
            w2 = lambda i: work[:, i]
            act.wait_ge(chain, 4)
            nc.scalar.activation(w2(2), w2(1), ACT.Exp).then_inc(chain_act, 1)
            nc.scalar.activation(w2(3), w2(4), ACT.Exp).then_inc(chain_act, 1)
            nc.scalar.activation(al_row[:], al_row[:], ACT.Exp).then_inc(chain_act, 1)
            act.wait_ge(chain, 5)
            nc.scalar.activation(w2(5), w2(4), ACT.Ln).then_inc(chain_act, 1)
            act.wait_ge(chain, 9)
            sc = out_sc[:].rearrange("p q h s t -> p s q h t")
            for s, i in ((2, 5), (3, 6), (4, 7)):
                for q in range(NQ):
                    nc.scalar.activation(sc[:, s, q], work[:, i, q * QT:(q + 1) * QT, :].rearrange("p t h -> p h t"),
                                         ACT.Exp).then_inc(chain_act, 1)

        @block.vector
        def _(dve):
            dve.wait_ge(cond_tanh_ready, 1)
            nc.vector.scalar_tensor_tensor(cond[:], cond_tanh[:], 1.0, cond[:], ALU.add, ALU.mult).then_inc(cond_tanh_ready, 1)
            dve.wait_ge(cond_tanh_ready, 2)
            nc.vector.tensor_scalar(cond[:], cond[:], 0.5, None, ALU.mult).then_inc(cond_ready, 1)
            dve.wait_ge(wab_loaded, 16)
            nc.vector.tensor_copy(wab_hi[:], wab[:]).then_inc(wab_hi_ready, 1)
            dve.wait_ge(wab_hi_ready, 1)
            nc.vector.tensor_tensor(wab_lo[:], wab[:], wab_hi[:].bitcast(F32), ALU.subtract).then_inc(wab_lo_ready, 1)
            dve.wait_ge(small_loaded, 48)

            def add_bias(j):
                dve.wait_ge(part_done, j + 1)
                row = slice(j * D, (j + 1) * D)
                nc.vector.tensor_tensor(mod_row[:, row], p_mod[:].rearrange("a n w -> a (n w)"), bias_row[:, row],
                                        ALU.add).then_inc(part_added, 1)
                if j in (1, 2, 4, 5):
                    dve.wait_ge(part_added, j + 1)
                    nc.vector.tensor_scalar(mod_row[:, row], mod_row[:, row], 1.0, None, ALU.add).then_inc(part_fixed, 1)

            add_bias(0)
            add_bias(1)
            for q in range(NQ):
                if q >= 1:
                    dve.wait_ge(hm_stored, 16 * q)
                    dve.wait_ge(ab_done, QT * q)
                for k in range(KT):
                    n = KT * q + k
                    dve.wait_ge(x_mod, n + 1)
                    nc.vector.tensor_copy(hm[:, 0, k, :], hm_f[:, n % 2, :]).then_inc(hm_hi, 1)
                    dve.wait_ge(hm_hi, n + 1)
                    nc.vector.tensor_tensor(hm[:, 1, k, :], hm_f[:, n % 2, :], hm[:, 0, k, :].bitcast(F32),
                                            ALU.subtract).then_inc(hm_lo, 1)
                add_bias(q + 2)
                for t in range(QT):
                    n = QT * q + t
                    dve.wait_ge(ab_done, n + 1)
                    nc.vector.tensor_copy(ab[:, n, :], p_ab[:, n % 2, 0:2 * H]).then_inc(ab_saved, 1)
            W = lambda i: work[:, i]
            flat = lambda i: work[:, i].rearrange("p t h -> p (t h)")
            dve.wait_ge(ab_saved, NT)
            a_part, b_part = ab[:, :, 0:H], ab[:, :, H:2 * H]
            nc.vector.tensor_tensor(W(0), a_part, dt_row[:].unsqueeze(1).to_broadcast([P, NT, H]), ALU.add).then_inc(chain, 1)
            dve.wait_ge(chain, 1)
            nc.vector.tensor_scalar(W(1), W(0), -1.0, None, ALU.mult).then_inc(chain, 1)
            nc.vector.tensor_scalar(W(4), b_part, -1.0, 80.0, ALU.mult, ALU.min).then_inc(chain, 1)
            dve.wait_ge(chain, 3)
            nc.vector.tensor_tensor(W(1), W(0), W(1), ALU.min).then_inc(chain, 1)
            dve.wait_ge(chain_act, 3)
            nc.vector.tensor_scalar(W(4), W(2), 1.0, None, ALU.add).then_inc(chain, 1)
            dve.wait_ge(chain, 5)
            dve.wait_ge(chain_act, 4)
            base = 4
            nc.vector.tensor_scalar(W(6), W(4), -1.0, 1e-30, ALU.add, ALU.max).then_inc(part_fixed, 1)
            dve.wait_ge(part_fixed, base + 1)
            nc.vector.reciprocal(W(7), W(6)).then_inc(part_fixed, 1)
            dve.wait_ge(part_fixed, base + 2)
            nc.vector.tensor_tensor(W(7), W(7), W(2), ALU.mult).then_inc(part_fixed, 1)
            nc.vector.tensor_scalar(W(6), W(6), 1e-30, None, ALU.is_le).then_inc(part_fixed, 1)
            dve.wait_ge(part_fixed, base + 4)
            nc.vector.tensor_tensor(W(7), W(7), W(5), ALU.mult).then_inc(part_fixed, 1)
            nc.vector.tensor_tensor(W(6), W(6), W(2), ALU.mult).then_inc(part_fixed, 1)
            dve.wait_ge(part_fixed, base + 6)
            nc.vector.tensor_tensor(W(7), W(7), W(6), ALU.add).then_inc(part_fixed, 1)
            nc.vector.tensor_scalar(W(0), W(0), 0.0, None, ALU.max).then_inc(part_fixed, 1)
            dve.wait_ge(part_fixed, base + 8)
            nc.vector.tensor_tensor(W(7), W(7), W(0), ALU.add).then_inc(chain, 1)
            dve.wait_ge(chain, 6)
            nc.vector.tensor_scalar(W(7), W(7), -1.0, None, ALU.mult).then_inc(part_fixed, 1)
            dve.wait_ge(part_fixed, base + 9)
            nc.vector.tensor_tensor(W(0), W(7), al_row[:].unsqueeze(1).to_broadcast([P, NT, H]), ALU.mult).then_inc(chain, 1)
            nc.vector.tensor_scalar(W(3), W(3), 1.0, None, ALU.add).then_inc(part_fixed, 1)
            dve.wait_ge(part_fixed, base + 10)
            nc.vector.reciprocal(W(1), W(3)).then_inc(part_fixed, 1)
            dve.wait_ge(cum_done, 2)
            nc.vector.tensor_copy(flat(5), p_cum[:, 0:NT * H]).then_inc(part_fixed, 1)
            nc.vector.tensor_copy(flat(7), p_tot[:, 0:NT * H]).then_inc(chain, 1)
            dve.wait_ge(part_fixed, base + 12)
            dve.wait_ge(chain, 8)
            nc.vector.tensor_tensor(W(6), W(7), W(5), ALU.subtract).then_inc(chain, 1)
            sc = out_sc[:].rearrange("p q h s t -> p s q h t")
            nc.vector.tensor_scalar(W(4), W(1), 0.5, None, ALU.mult).then_inc(part_fixed, 1)
            dve.wait_ge(part_fixed, base + 13)
            for s, i in ((0, 0), (1, 1), (5, 5), (6, 4)):
                for q in range(NQ):
                    nc.vector.tensor_copy(sc[:, s, q], work[:, i, q * QT:(q + 1) * QT, :].rearrange("p t h -> p h t")).then_inc(part_fixed, 1)
            dve.wait_ge(part_fixed, base + 29)
            dve.wait_ge(chain_act, 16)
            nc.vector.memset(bias_row[:, 0:1], 0.0).then_inc(chain, 91)


PRIME = 2
SPLIT_PIECES = 4
PK = KT // SPLIT_PIECES
LEVELS = 7


def deltanet_phase(nc, hm_split, gate_scalars, w_in, conv_w, norm_g, mixed):
    with ExitStack() as ctx:
        sb, ps, sem = allocators(nc, ctx, "delta")
        hm = sb("hm", [P, 2, 2, KT, QW], F32R)
        w_raw = [sb(f"w_raw{i}", [P, PK, 4, P]) for i in range(2)]
        w_hi = [sb(f"w_hi{i}", [P, KT, 4, P], F32R) for i in range(2)]
        w_lo = [sb(f"w_lo{i}", [P, KT, 4, P], F32R) for i in range(2)]
        conv_in = sb("conv_in", [P, 3, TAPS - 1 + QW])
        conv_acc = sb("conv_acc", [P, 3, QW])
        tanh = sb("tanh", [P, 2, QW])
        act_q, act_k, act_v = (sb(f"act_{n}", [P, QW]) for n in "qkv")
        act_z = [sb(f"act_z{i}", [P, QW]) for i in range(2)]
        halo = sb("halo", [P, H, 3, TAPS - 1])
        conv_all = sb("conv_all", [P, H, 3, TAPS])
        conv_w_item = [sb(f"conv_w_item{i}", [P, 3, TAPS]) for i in range(2)]
        scal_all = sb("scal_all", [P, ITEMS, NSC, QT])
        scal = [sb(f"scal{i}", [P, NSC, QT]) for i in range(2)]
        state = sb("state", [P, H, P])
        ident = sb("ident", [P, P])
        upper = sb("upper", [P, P])
        level_mask = sb("level_mask", [P, LEVELS, P])
        half_norm_g = sb("half_norm_g", [P, 1])
        expo = sb("expo", [P, QW])
        decay = sb("decay", [P, QW])
        grow = sb("grow", [P, QW])
        q_grown = sb("q_grown", [P, QW])
        sq_k = sb("sq_k", [P, QW])
        sq_q = sb("sq_q", [P, QW])
        attn = sb("attn", [P, QW])
        lower = sb("lower", [P, QW])
        inv = sb("inv", [P, QW])
        inv_t = sb("inv_t", [P, QW])
        prod = sb("prod", [P, QW])
        k_beta = sb("k_beta", [P, QW])
        k_end = sb("k_end", [P, QW])
        v_beta = sb("v_beta", [P, QW])
        w_neg, v_new, o_norm = expo, sq_k, grow
        o_out = sb("o_out", [P, QW])
        sums = sb("sums", [P, 2, QT])
        r_qk = sb("r_qk", [P, 2, QT])
        half_neg = sb("half_neg", [P, 2, QT])
        four_eps = sb("four_eps", [P, 2, QT])
        br = sb("br", [P, QT])
        brg = sb("brg", [P, QT])
        kend_s = sb("kend_s", [P, QT])
        o_sum = sb("o_sum", [P, QT])
        rq = sb("rq", [P, QT])
        o_s = sb("o_s", [P, 3, QT])
        pa = [ps(f"pa{i}", [P, QW]) for i in range(2)]
        b0, b1, b2, b3, b4, b5 = (ps(f"b{i}", [P, QW]) for i in range(6))

        tiles = lambda t: t[:].rearrange("p (t n) -> p t n", t=QT)
        one = lambda t, i: t[:, i * P:(i + 1) * P]
        per_tile = lambda s: s.unsqueeze(2).to_broadcast([P, QT, P])
        LG, BETA, EG, EKD, ETOT, CUM, HBETA = range(NSC)

        plain = "hm_loaded w_loaded0 w_loaded1 setup_loaded consts passed".split()
        hm_loaded, w_loaded0, w_loaded1, setup_loaded, consts, passed = (sem(n) for n in plain)
        w_loaded = (w_loaded0, w_loaded1)
        primed = []

        def stage(name):
            primed.append(sem(name))
            return primed[-1]

        def stages(names):
            return [stage(n) for n in names.split()]

        hi_split = stages("hi_split0 hi_split1")
        lo_split = stages("lo_split0 lo_split1")
        projected = stages("projected_q projected_k projected_v projected_z")
        evacuated = stages("evacuated_q evacuated_k evacuated_v")
        halo_read = stages("halo_read_q halo_read_k halo_read_v")
        halo_saved = stages("halo_saved_q halo_saved_k halo_saved_v")
        tap = [stages(f"tap{j}_q tap{j}_k tap{j}_v") for j in range(TAPS)]
        tanh_done = stages("tanh_q tanh_k tanh_v tanh_z")
        silu_done = stages("silu_q silu_k silu_v silu_z")
        (scal_copied, conv_copied, k_tr, q_tr, v_tr, kk_gram, cum_rows, kq_gram, sq_k_done, sq_q_done, sums_done, eps_done,
         r_done, br_done, brg_done, kend_done, expo_done, decay_exp, decay_masked, grow_done, q_grown_done, br_rows,
         k_beta_done, k_end_done, v_beta_done, attn_done, lower_raw, lower_done) = stages(
            "scal_copied conv_copied k_tr q_tr v_tr kk_gram cum_rows kq_gram sq_k_done sq_q_done sums_done eps_done "
            "r_done br_done brg_done kend_done expo_done decay_exp decay_masked grow_done q_grown_done br_rows "
            "k_beta_done k_end_done v_beta_done attn_done lower_raw lower_done")
        level_p = stages(" ".join(f"level_p{s}" for s in range(LEVELS)))
        level_pm = stages(" ".join(f"level_pm{s}" for s in range(LEVELS)))
        level_q = [None] + stages(" ".join(f"level_q{s}" for s in range(1, LEVELS)))
        level_inv = stages(" ".join(f"level_inv{s}" for s in range(LEVELS)))
        level_tr = [None] + stages(" ".join(f"level_tr{s}" for s in range(1, LEVELS)))
        level_trc = [None] + stages(" ".join(f"level_trc{s}" for s in range(1, LEVELS)))
        w_mm, w_done, o_ready, o_sq, o_sum_done, o_c1, o_c2, o_c3, o_c4, o_c5, o_s_done, o_scaled, o_tr, o_done, out_stored = stages(
            "w_mm w_done o_ready o_sq o_sum_done o_c1 o_c2 o_c3 o_c4 o_c5 o_s_done o_scaled o_tr o_done out_stored")
        scan_v = stages(" ".join(f"scan_v{t}" for t in range(QT)))
        scan_vs = stages(" ".join(f"scan_vs{t}" for t in range(QT)))
        scan_s = stages(" ".join(f"scan_s{t}" for t in range(QT)))
        scan_st = stages(" ".join(f"scan_st{t}" for t in range(QT)))

        w_cols = w_in.rearrange("(k p) n -> p k n", p=P)
        block = ctx.enter_context(nc.Block())

        def through(i):
            return i + 1 + PRIME


        def all_items(eng, item):
            with eng.Fori(0, ITEMS // 2 - 1) as pair:
                for par in range(2):
                    item(pair * 2 + par, par, True, True)
            item(ITEMS - 2, 0, True, False)
            item(ITEMS - 1, 1, False, False)

        @block.sync
        def _(sp):
            for s in primed:
                sp.sem_inc(s, PRIME)
            sp.dma_start(scal_all[:].rearrange("p i s t -> p (i s t)"), gate_scalars).then_inc(setup_loaded, 16)
            with nc.allow_non_contiguous_dma(reason="one value on each partition"):
                for c in range(3):
                    for j in range(TAPS):
                        sp.dma_start(conv_all[:, :, c, j],
                                     conv_w[j, c * D:(c + 1) * D].rearrange("(h p) -> p h", p=P)).then_inc(setup_loaded, 16)
                sp.dma_start(half_norm_g[:], norm_g.rearrange("a p -> p a")).then_inc(setup_loaded, 16)

            def load_weights(i, head):
                for j in range(SPLIT_PIECES):
                    sp.wait_ge(hi_split[j % 2], 2 * i + (j // 2) + PRIME)
                    sp.wait_ge(lo_split[j % 2], 2 * i + (j // 2) + PRIME)
                    sp.sem_inc(passed, 1)
                    for c in range(4):
                        sp.dma_start(w_raw[j % 2][:, :, c, :],
                                     w_cols[:, j * PK:(j + 1) * PK, bass.ds(head * P + c * D, P)]).then_inc(w_loaded[j % 2], 16)

            def store(i):
                sp.wait_ge(o_done, through(i))
                sp.sem_inc(passed, 1)
                sp.dma_start(mixed[bass.ds(i, 1)].rearrange("a p w -> p (a w)"), o_out[:]).then_inc(out_stored, 16)

            hm_f = hm[:].bitcast(F32)
            sp.dma_start(hm_f[:, 0], hm_split[0]).then_inc(hm_loaded, 16)
            load_weights(0, 0)
            load_weights(1, 1)
            with sp.Fori(0, NQ - 1) as q:
                sp.wait_ge(hm_loaded, 16 * (q + 1))
                sp.wait_ge(projected[3], H * q + PRIME)
                sp.sem_inc(passed, 1)
                sp.dma_start(hm_f[:, bass.ds((q + 1) & 1, 1)].rearrange("p a s k w -> p (a s k w)"),
                             hm_split[bass.ds(q + 1, 1)].rearrange("a p s k w -> p (a s k w)")).then_inc(hm_loaded, 16)
                with sp.Fori(0, H) as h:
                    load_weights(q * H + h + 2, (h + 2) & (H - 1))
                    store(q * H + h)
            for h in range(H):
                if h < H - 2:
                    load_weights((NQ - 1) * H + h + 2, h + 2)
                store((NQ - 1) * H + h)
            sp.wait_ge(out_stored, 16 * ITEMS + PRIME)

        @block.gpsimd
        def _(pool):
            nc.gpsimd.memset(ident[:], 0.0).then_inc(consts, 1)
            nc.gpsimd.memset(upper[:], 1.0).then_inc(consts, 1)
            nc.gpsimd.memset(half_neg[:], -0.5).then_inc(consts, 1)
            nc.gpsimd.memset(four_eps[:], 4e-6)
            nc.gpsimd.memset(state[:], 0.0).then_inc(consts, 1)
            nc.gpsimd.memset(halo[:], 0.0).then_inc(consts, 1)
            nc.gpsimd.memset(level_mask[:], -1.0).then_inc(consts, 1)
            pool.wait_ge(consts, 6)
            nc.gpsimd.affine_select(out=ident[:], in_=ident[:], compare_op=ALU.not_equal, fill=1.0, base=0,
                                    pattern=[[-1, P]], channel_multiplier=1).then_inc(consts, 1)
            nc.gpsimd.affine_select(out=upper[:], in_=upper[:], compare_op=ALU.is_ge, fill=0.0, base=0,
                                    pattern=[[1, P]], channel_multiplier=-1).then_inc(consts, 1)
            n = 8
            for s in range(LEVELS):
                b = 1 << s
                pairs = P // (2 * b)
                m = level_mask[:, s, :].rearrange("p (a two c) -> p a two c", two=2, c=b)
                for pat, base, mult in (([[0, pairs], [-1, 2], [0, b]], 0, 0),
                                        ([[-2 * b, pairs], [0, 2], [0, b]], -b, 1),
                                        ([[2 * b, pairs], [0, 2], [0, b]], 2 * b - 1, -1)):
                    pool.wait_ge(consts, n)
                    nc.gpsimd.affine_select(out=m, in_=m, compare_op=ALU.is_ge, fill=0.0, base=base, pattern=pat,
                                            channel_multiplier=mult).then_inc(consts, 1)
                    n += 1
            pool.wait_ge(setup_loaded, 16 * 14)
            nc.gpsimd.tensor_scalar(half_norm_g[:], half_norm_g[:], 0.5, 1.0, ALU.mult, ALU.mult).then_inc(consts, 1)

            def copy_taps(i, par):
                pool.wait_ge(setup_loaded, 16 * 14)
                pool.wait_ge(tap[3][2], through(i - 2))
                nc.gpsimd.tensor_copy(conv_w_item[par][:].rearrange("p c t -> p (c t)"),
                                      conv_all[:, bass.ds(i & (H - 1), 1)].rearrange("p a c t -> p (a c t)")).then_inc(conv_copied, 1)

            def copy_scalars(i, par):
                pool.wait_ge(setup_loaded, 16 * 14)
                pool.wait_ge(o_done, through(i - 2))
                nc.gpsimd.tensor_copy(scal[par][:].rearrange("p s t -> p (s t)"),
                                      scal_all[:, bass.ds(i, 1)].rearrange("p a s t -> p (a s t)")).then_inc(scal_copied, 1)

            def split_low(i, par, j):
                if j == 0:
                    pool.wait_ge(projected[3], through(i - 2))
                pool.wait_ge(w_loaded[j % 2], 64 * (2 * i + j // 2 + 1))
                pool.wait_ge(hi_split[j % 2], 2 * i + j // 2 + 1 + PRIME)
                part = slice(j * PK, (j + 1) * PK)
                nc.gpsimd.tensor_tensor(w_lo[par][:, part].rearrange("p k c n -> p (k c n)"),
                                        w_raw[j % 2][:].rearrange("p k c n -> p (k c n)"),
                                        w_hi[par][:, part].bitcast(F32).rearrange("p k c n -> p (k c n)"),
                                        ALU.subtract).then_inc(lo_split[j % 2], 1)

            def item(i, par, more, ahead):
                V = through(i)
                pool.wait_ge(sums_done, V)
                nc.gpsimd.tensor_tensor(sums[:], sums[:], four_eps[:], ALU.add).then_inc(eps_done, 1)
                pool.wait_ge(eps_done, V)
                pool.wait_ge(o_c1, V - 1)
                pool.wait_ge(lower_raw, V - 1)
                nc.gpsimd.tensor_tensor(r_qk[:], sums[:], half_neg[:], ALU.pow).then_inc(r_done, 1)
                pool.wait_ge(r_done, V)
                pool.wait_ge(scal_copied, V)
                pool.wait_ge(br_rows, V - 1)
                nc.gpsimd.tensor_tensor(br[:], r_qk[:, 1], scal[par][:, BETA], ALU.mult).then_inc(br_done, 1)
                pool.wait_ge(k_end_done, V - 1)
                nc.gpsimd.tensor_tensor(kend_s[:], r_qk[:, 1], scal[par][:, EKD], ALU.mult).then_inc(kend_done, 1)
                pool.wait_ge(br_done, V)
                pool.wait_ge(k_beta_done, V - 1)
                nc.gpsimd.tensor_tensor(brg[:], br[:], scal[par][:, EG], ALU.mult).then_inc(brg_done, 1)
                pool.wait_ge(consts, 3)
                pool.wait_ge(decay_exp, V)
                nc.gpsimd.affine_select(out=tiles(decay), in_=tiles(decay), compare_op=ALU.is_ge, fill=0.0, base=0,
                                        pattern=[[0, QT], [1, P]], channel_multiplier=-1).then_inc(decay_masked, 1)
                if ahead:
                    for j in range(SPLIT_PIECES):
                        split_low(i + 2, par, j)
                if more:
                    copy_scalars(i + 1, 1 - par)
                if ahead:
                    copy_taps(i + 2, par)
                pool.wait_ge(consts, 3)
                pool.wait_ge(r_done, V)
                nc.gpsimd.tensor_scalar(rq[:], r_qk[:, 0], P ** -0.5, 1.0, ALU.mult, ALU.mult).then_inc(o_c1, 1)
                pool.wait_ge(o_c1, V)
                nc.gpsimd.tensor_tensor(o_s[:, 0], rq[:], rq[:], ALU.mult).then_inc(o_c2, 1)
                pool.wait_ge(o_c2, V)
                pool.wait_ge(o_sum_done, V)
                nc.gpsimd.tensor_tensor(o_s[:, 1], o_s[:, 0], o_sum[:], ALU.mult).then_inc(o_c3, 1)
                pool.wait_ge(consts, 3)
                pool.wait_ge(o_c3, V)
                nc.gpsimd.tensor_scalar(o_s[:, 0], o_s[:, 1], 1.0 / P, 1e-6, ALU.mult, ALU.add).then_inc(o_c4, 1)
                pool.wait_ge(o_c4, V)
                nc.gpsimd.tensor_tensor(o_s[:, 1], o_s[:, 0], half_neg[:, 0], ALU.pow).then_inc(o_c5, 1)
                pool.wait_ge(o_c5, V)
                pool.wait_ge(o_scaled, V - 1)
                nc.gpsimd.tensor_tensor(o_s[:, 2], o_s[:, 1], rq[:], ALU.mult).then_inc(o_s_done, 1)

            copy_taps(0, 0)
            copy_taps(1, 1)
            for j in range(SPLIT_PIECES):
                split_low(0, 0, j)
            copy_scalars(0, 0)
            for j in range(SPLIT_PIECES):
                split_low(1, 1, j)
            all_items(pool, item)

        @block.scalar
        def _(act):
            def split_high(i, par, j):
                act.wait_ge(projected[3], through(i - 2))
                act.wait_ge(lo_split[j % 2], 2 * i + j // 2 + PRIME)
                act.wait_ge(w_loaded[j % 2], 64 * (2 * i + j // 2 + 1))
                nc.scalar.activation(w_hi[par][:, j * PK:(j + 1) * PK].rearrange("p k c n -> p (k c n)"),
                                     w_raw[j % 2][:].rearrange("p k c n -> p (k c n)"), ACT.Copy).then_inc(hi_split[j % 2], 1)

            def evacuate(i, c):
                V = through(i)
                head = bass.ds(i & (H - 1), 1)
                act.wait_ge(consts, 6)
                act.wait_ge(halo_saved[c], V - 1)
                act.wait_ge(tap[3][c], V - 1)
                nc.scalar.activation(conv_in[:, c, 0:TAPS - 1], halo[:, head, c, :].rearrange("p a t -> p (a t)"),
                                     ACT.Copy).then_inc(halo_read[c], 1)
                act.wait_ge(projected[c], V)
                nc.scalar.activation(conv_in[:, c, TAPS - 1:], pa[c % 2][:], ACT.Copy).then_inc(evacuated[c], 1)
                act.wait_ge(consts, 6)
                act.wait_ge(evacuated[c], V)
                act.wait_ge(halo_read[c], V)
                nc.scalar.activation(halo[:, head, c, :].rearrange("p a t -> p (a t)"), conv_in[:, c, QW:],
                                     ACT.Copy).then_inc(halo_saved[c], 1)

            def tanh_half(i, c):
                V = through(i)
                act.wait_ge(silu_done[c - 2 if c >= 2 else c + 2], V if c >= 2 else V - 1)
                if c < 3:
                    act.wait_ge(tap[3][c], V)
                    src = conv_acc[:, c, :]
                else:
                    act.wait_ge(projected[3], V)
                    src = pa[1][:]
                nc.scalar.activation(tanh[:, c % 2, :], src, ACT.Tanh, scale=0.5).then_inc(tanh_done[c], 1)

            def take_transpose(i, s):
                V = through(i)
                act.wait_ge(level_tr[s], V)
                if s == 1:
                    act.wait_ge(scan_v[QT - 1], V - 1)
                else:
                    act.wait_ge(level_q[s - 1], V)
                nc.scalar.activation(inv_t[:], b2[:], ACT.Copy).then_inc(level_trc[s], 1)

            def item(i, par, more, ahead):
                V = through(i)
                act.wait_ge(k_tr, V)
                act.wait_ge(o_ready, V - 1)
                nc.scalar.activation(sq_k[:], b0[:], ACT.Square).then_inc(sq_k_done, 1)
                act.wait_ge(q_tr, V)
                act.wait_ge(o_sum_done, V - 1)
                nc.scalar.activation(sq_q[:], b5[:], ACT.Square).then_inc(sq_q_done, 1)
                act.wait_ge(expo_done, V)
                act.wait_ge(o_tr, V - 1)
                nc.scalar.activation(grow[:], b4[:], ACT.Exp).then_inc(grow_done, 1)
                act.wait_ge(lower_raw, V - 1)
                act.wait_ge(attn_done, V - 1)
                nc.scalar.activation(decay[:], expo[:], ACT.Exp).then_inc(decay_exp, 1)
                if ahead:
                    split_high(i + 2, par, 0)
                take_transpose(i, 1)
                if more:
                    evacuate(i + 1, 0)
                take_transpose(i, 2)
                if ahead:
                    split_high(i + 2, par, 1)
                take_transpose(i, 3)
                take_transpose(i, 4)
                if ahead:
                    split_high(i + 2, par, 2)
                take_transpose(i, 5)
                if more:
                    evacuate(i + 1, 1)
                take_transpose(i, 6)
                if more:
                    tanh_half(i + 1, 0)
                if ahead:
                    split_high(i + 2, par, 3)
                act.wait_ge(w_mm, V)
                act.wait_ge(decay_exp, V)
                nc.scalar.activation(w_neg[:], b4[:], ACT.Copy, scale=-1.0).then_inc(w_done, 1)
                if more:
                    tanh_half(i + 1, 1)
                    evacuate(i + 1, 2)
                act.wait_ge(o_ready, V)
                act.wait_ge(sums_done, V)
                nc.scalar.activation(sq_q[:], b3[:], ACT.Square).then_inc(o_sq, 1)
                if more:
                    tanh_half(i + 1, 2)
                    tanh_half(i + 1, 3)

            for j in range(SPLIT_PIECES):
                split_high(0, 0, j)
            act.wait_ge(consts, 9)
            evacuate(0, 0)
            evacuate(0, 1)
            tanh_half(0, 0)
            evacuate(0, 2)
            tanh_half(0, 1)
            tanh_half(0, 2)
            tanh_half(0, 3)
            for j in range(SPLIT_PIECES):
                split_high(1, 1, j)
            all_items(act, item)

        @block.vector
        def _(dve):
            def convolve(i, par, c, j):
                V = through(i)
                w = conv_w_item[par][:, c, j:j + 1]
                if j == 0:
                    dve.wait_ge(evacuated[c], V)
                    dve.wait_ge(halo_read[c], V)
                    dve.wait_ge(conv_copied, V)
                    dve.wait_ge(silu_done[c], V - 1)
                    nc.vector.tensor_scalar(conv_acc[:, c, :], conv_in[:, c, 0:QW], w, None, ALU.mult).then_inc(tap[0][c], 1)
                else:
                    dve.wait_ge(tap[j - 1][c], V)
                    nc.vector.scalar_tensor_tensor(conv_acc[:, c, :], conv_in[:, c, j:j + QW], w, conv_acc[:, c, :],
                                                   ALU.mult, ALU.add).then_inc(tap[j][c], 1)

            def silu(i, par, c):
                V = through(i)
                dve.wait_ge(tanh_done[c], V)
                if c == 0:
                    dve.wait_ge(q_tr, V - 1)
                    dve.wait_ge(kq_gram, V - 1)
                    dve.wait_ge(q_grown_done, V - 1)
                elif c == 1:
                    dve.wait_ge(kq_gram, V - 1)
                elif c == 2:
                    dve.wait_ge(v_tr, V - 1)
                else:
                    dve.wait_ge(o_done, V - 2)
                out = (act_q, act_k, act_v, act_z[par])[c]
                src = conv_acc[:, c, :] if c < 3 else pa[1][:]
                nc.vector.scalar_tensor_tensor(out[:], tanh[:, c % 2, :], 1.0, src, ALU.add, ALU.mult).then_inc(silu_done[c], 1)

            def merge(i, s):
                V = through(i)
                dve.wait_ge(level_p[s], V)
                if s == 0:
                    dve.wait_ge(level_q[LEVELS - 1], V - 1)
                else:
                    dve.wait_ge(level_inv[s - 1], V)
                nc.vector.tensor_tensor(tiles(prod), tiles(b0), level_mask[:, s, :].unsqueeze(1).to_broadcast([P, QT, P]),
                                        ALU.mult).then_inc(level_pm[s], 1)

            def update(i, s):
                V = through(i)
                if s == 0:
                    dve.wait_ge(level_pm[0], V)
                    dve.wait_ge(level_tr[LEVELS - 1], V - 1)
                    nc.vector.tensor_tensor(tiles(inv), tiles(prod), ident[:].unsqueeze(1).to_broadcast([P, QT, P]),
                                            ALU.add).then_inc(level_inv[0], 1)
                elif s < LEVELS - 1:
                    dve.wait_ge(level_q[s], V)
                    nc.vector.tensor_tensor(inv[:], inv[:], b1[:], ALU.add).then_inc(level_inv[s], 1)
                else:
                    dve.wait_ge(level_q[s], V)
                    dve.wait_ge(level_trc[s], V)
                    nc.vector.tensor_tensor(inv_t[:], inv_t[:], b1[:], ALU.add).then_inc(level_inv[s], 1)

            def new_values(i, t):
                V = through(i)
                dve.wait_ge(scan_v[t], V)
                dve.wait_ge(sums_done, V)
                nc.vector.tensor_copy(one(v_new, t), one(b0, t)).then_inc(scan_vs[t], 1)

            def new_state(i, par, t):
                V = through(i)
                S = state[:, bass.ds(i & (H - 1), 1), :].rearrange("p a n -> p (a n)")
                dve.wait_ge(scan_s[t], V)
                if t == 0:
                    dve.wait_ge(scan_st[QT - 1], V - 1)
                else:
                    dve.wait_ge(scan_st[t - 1], V)
                nc.vector.scalar_tensor_tensor(S, S, scal[par][:, ETOT, t:t + 1], one(b1, t), ALU.mult, ALU.add).then_inc(scan_st[t], 1)

            def item(i, par, more, ahead):
                V = through(i)
                nxt = 1 - par
                dve.wait_ge(cum_rows, V)
                dve.wait_ge(scal_copied, V)
                dve.wait_ge(scan_v[QT - 1], V - 1)
                for t in range(QT):
                    cum = scal[par][:, CUM, t:t + 1]
                    last = nc.vector.tensor_scalar(one(expo, t), one(b4, t), cum, cum, ALU.min, ALU.subtract)
                last.then_inc(expo_done, 1)
                dve.wait_ge(sq_k_done, V)
                dve.wait_ge(r_done, V - 1)
                nc.vector.tensor_reduce(sums[:, 1], tiles(sq_k), AX.X, ALU.add)
                dve.wait_ge(sq_q_done, V)
                nc.vector.tensor_reduce(sums[:, 0], tiles(sq_q), AX.X, ALU.add).then_inc(sums_done, 1)
                dve.wait_ge(v_tr, V)
                dve.wait_ge(scan_v[QT - 1], V - 1)
                nc.vector.tensor_tensor(tiles(v_beta), tiles(b1), per_tile(scal[par][:, HBETA]), ALU.mult).then_inc(v_beta_done, 1)
                dve.wait_ge(kend_done, V)
                dve.wait_ge(k_tr, V)
                dve.wait_ge(scan_s[QT - 1], V - 1)
                nc.vector.tensor_tensor(tiles(k_end), tiles(b0), per_tile(kend_s[:]), ALU.mult).then_inc(k_end_done, 1)
                dve.wait_ge(brg_done, V)
                dve.wait_ge(w_mm, V - 1)
                nc.vector.tensor_tensor(tiles(k_beta), tiles(b0), per_tile(brg[:]), ALU.mult).then_inc(k_beta_done, 1)
                dve.wait_ge(grow_done, V)
                dve.wait_ge(o_ready, V - 1)
                nc.vector.tensor_tensor(q_grown[:], act_q[:], grow[:], ALU.mult).then_inc(q_grown_done, 1)
                dve.wait_ge(kk_gram, V)
                dve.wait_ge(decay_masked, V)
                dve.wait_ge(level_p[LEVELS - 1], V - 1)
                for t in range(QT):
                    last = nc.vector.scalar_tensor_tensor(one(lower, t), one(b2, t), r_qk[:, 1, t:t + 1], one(decay, t),
                                                          ALU.mult, ALU.mult)
                last.then_inc(lower_raw, 1)
                dve.wait_ge(br_rows, V)
                dve.wait_ge(lower_raw, V)
                nc.vector.tensor_tensor(lower[:], lower[:], b5[:], ALU.mult).then_inc(lower_done, 1)
                dve.wait_ge(kq_gram, V)
                for t in range(QT):
                    last = nc.vector.scalar_tensor_tensor(one(attn, t), one(b3, t), r_qk[:, 1, t:t + 1], one(decay, t),
                                                          ALU.mult, ALU.mult)
                last.then_inc(attn_done, 1)
                merge(i, 0)
                update(i, 0)
                for s in range(1, LEVELS):
                    merge(i, s)
                    if more:
                        convolve(i + 1, nxt, (s - 1) // 4, (s - 1) % 4)
                    update(i, s)
                if more:
                    silu(i + 1, nxt, 0)
                    convolve(i + 1, nxt, 1, 2)
                    convolve(i + 1, nxt, 1, 3)
                new_values(i, 0)
                new_state(i, par, 0)
                new_values(i, 1)
                new_state(i, par, 1)
                if more:
                    silu(i + 1, nxt, 1)
                new_values(i, 2)
                new_state(i, par, 2)
                if more:
                    convolve(i + 1, nxt, 2, 0)
                new_values(i, 3)
                new_state(i, par, 3)
                if more:
                    convolve(i + 1, nxt, 2, 1)
                dve.wait_ge(o_sq, V)
                dve.wait_ge(o_c3, V - 1)
                nc.vector.tensor_reduce(o_sum[:], tiles(sq_q), AX.X, ALU.add).then_inc(o_sum_done, 1)
                if more:
                    convolve(i + 1, nxt, 2, 2)
                dve.wait_ge(o_s_done, V)
                dve.wait_ge(q_grown_done, V)
                nc.vector.tensor_tensor(tiles(o_norm), tiles(b3), per_tile(o_s[:, 2]), ALU.mult).then_inc(o_scaled, 1)
                if more:
                    convolve(i + 1, nxt, 2, 3)
                dve.wait_ge(o_tr, V)
                dve.wait_ge(silu_done[3], V)
                dve.wait_ge(out_stored, 16 * i + PRIME)
                nc.vector.scalar_tensor_tensor(o_out[:], b2[:], half_norm_g[:], act_z[par][:], ALU.mult, ALU.mult).then_inc(o_done, 1)
                if more:
                    silu(i + 1, nxt, 2)
                    silu(i + 1, nxt, 3)

            for c in range(3):
                for j in range(TAPS):
                    convolve(0, 0, c, j)
                silu(0, 0, c)
            silu(0, 0, 3)
            dve.wait_ge(consts, 8 + 3 * LEVELS + 1)
            all_items(dve, item)

        @block.tensor
        def _(pe):
            def project(i, par, first, end):
                V = through(i)
                half = bass.ds((i >> 3) & 1, 1)
                for step in range(first, end):
                    c, k = divmod(step, KT)
                    if step == 0:
                        for b in range(2):
                            pe.wait_ge(hi_split[b], 2 * i + 2 + PRIME)
                            pe.wait_ge(lo_split[b], 2 * i + 2 + PRIME)
                        pe.wait_ge(hm_loaded, 16 * ((i >> 3) + 1))
                    if k == 0:
                        if c == 0:
                            pe.wait_ge(evacuated[2], V - 1)
                        elif c == 1:
                            pe.wait_ge(silu_done[3], V - 1)
                        else:
                            pe.wait_ge(evacuated[c - 2], V)
                    x_hi = hm[:, half, 0, k, :].rearrange("p a w -> p (a w)")
                    x_lo = hm[:, half, 1, k, :].rearrange("p a w -> p (a w)")
                    nc.tensor.matmul(pa[c % 2][:], w_hi[par][:, k, c, :], x_hi, start=(k == 0), stop=False)
                    nc.tensor.matmul(pa[c % 2][:], w_hi[par][:, k, c, :], x_lo, start=False, stop=False)
                    last = nc.tensor.matmul(pa[c % 2][:], w_lo[par][:, k, c, :], x_hi, start=False, stop=(k == KT - 1))
                    if k == KT - 1:
                        last.then_inc(projected[c], 1)

            def item(i, par, more, ahead):
                V = through(i)

                def fill(first, end):
                    if more:
                        project(i + 1, 1 - par, first, end)

                def each(out, lhs, rhs):
                    for t in range(QT):
                        last = nc.tensor.matmul(one(out, t), one(lhs, t), one(rhs, t), start=True, stop=True)
                    return last

                def transposes(out, src):
                    for t in range(QT):
                        last = nc.tensor.transpose(one(out, t), one(src, t), ident[:])
                    return last

                pe.wait_ge(silu_done[1], V)
                pe.wait_ge(scan_vs[QT - 1], V - 1)
                transposes(b0, act_k).then_inc(k_tr, 1)
                pe.wait_ge(scal_copied, V)
                pe.wait_ge(w_done, V - 1)
                for t in range(QT):
                    last = nc.tensor.matmul(one(b4, t), scal[par][:, LG, t:t + 1].to_broadcast([P, P]), upper[:],
                                            start=True, stop=True)
                last.then_inc(cum_rows, 1)
                pe.wait_ge(silu_done[0], V)
                pe.wait_ge(lower_done, V - 1)
                transposes(b5, act_q).then_inc(q_tr, 1)
                pe.wait_ge(o_done, V - 1)
                each(b2, act_k, act_k).then_inc(kk_gram, 1)
                pe.wait_ge(silu_done[2], V)
                pe.wait_ge(scan_st[QT - 1], V - 1)
                transposes(b1, act_v).then_inc(v_tr, 1)
                pe.wait_ge(o_sq, V - 1)
                pe.wait_ge(o_scaled, V - 1)
                each(b3, act_k, act_q).then_inc(kq_gram, 1)
                fill(0, 4)
                pe.wait_ge(br_done, V)
                pe.wait_ge(sq_q_done, V)
                for t in range(QT):
                    last = nc.tensor.matmul(one(b5, t), br[:, t:t + 1].to_broadcast([P, P]), ident[:], start=True, stop=True)
                last.then_inc(br_rows, 1)
                fill(4, 7)
                pe.wait_ge(lower_done, V)
                pe.wait_ge(k_beta_done, V)
                for t in range(QT):
                    last = nc.tensor.matmul(one(b0, t), one(lower, t), ident[:], start=True, stop=True)
                last.then_inc(level_p[0], 1)
                fill(7, 8)
                for s in range(1, LEVELS):
                    pe.wait_ge(level_inv[s - 1], V)
                    each(b0, lower, inv).then_inc(level_p[s], 1)
                    if s == 1:
                        pe.wait_ge(lower_raw, V)
                    else:
                        pe.wait_ge(level_trc[s - 1], V)
                    transposes(b2, inv).then_inc(level_tr[s], 1)
                    fill(6 + 2 * s, 7 + 2 * s)
                    pe.wait_ge(level_pm[s], V)
                    pe.wait_ge(level_trc[s], V)
                    if s == 1:
                        pe.wait_ge(v_beta_done, V)
                    if s < LEVELS - 1:
                        each(b1, inv_t, prod).then_inc(level_q[s], 1)
                    else:
                        each(b1, prod, inv_t).then_inc(level_q[s], 1)
                    fill(7 + 2 * s, 8 + 2 * s)
                pe.wait_ge(level_inv[LEVELS - 1], V)
                pe.wait_ge(grow_done, V)
                each(b4, k_beta, inv_t).then_inc(w_mm, 1)
                fill(20, 21)
                pe.wait_ge(w_done, V)
                pe.wait_ge(q_grown_done, V)
                pe.wait_ge(attn_done, V)
                pe.wait_ge(k_end_done, V)
                S = state[:, bass.ds(i & (H - 1), 1), :].rearrange("p a n -> p (a n)")
                for t in range(QT):
                    if t == 0:
                        pe.wait_ge(scan_st[QT - 1], V - 1)
                    else:
                        pe.wait_ge(scan_st[t - 1], V)
                    nc.tensor.matmul(one(b0, t), one(inv_t, t), one(v_beta, t), start=True, stop=False)
                    nc.tensor.matmul(one(b0, t), one(w_neg, t), S, start=False, stop=True).then_inc(scan_v[t], 1)
                    nc.tensor.matmul(one(b3, t), one(q_grown, t), S, start=True, stop=False)
                    fill(21 + t, 22 + t)
                    pe.wait_ge(scan_vs[t], V)
                    nc.tensor.matmul(one(b1, t), one(k_end, t), one(v_new, t), start=True, stop=True).then_inc(scan_s[t], 1)
                    last = nc.tensor.matmul(one(b3, t), one(attn, t), one(v_new, t), start=False, stop=True)
                last.then_inc(o_ready, 1)
                fill(25, 30)
                pe.wait_ge(o_scaled, V)
                transposes(b2, o_norm).then_inc(o_tr, 1)
                fill(30, 32)

            project(0, 0, 0, 4 * KT)
            pe.wait_ge(consts, 8 + 3 * LEVELS + 1)
            all_items(pe, item)


ALPHA = 2.0 ** 0.25


def mixer_output_phase(nc, mixed, w_out, x, mod_rows, ln1_g, ln1_b, w_grp, w_exp, x_scaled, hf, logits):
    with ExitStack() as ctx:
        sb, ps, sem = allocators(nc, ctx, "mixout")
        wo_raw = [sb(f"wo_raw{i}", [P, D]) for i in range(2)]
        wo_hi = sb("wo_hi", [P, H, D], F32R)
        wo_lo = sb("wo_lo", [P, H, D], F32R)
        gate1, g_row, b_row, scale2, shift2 = (sb(n, [P, D]) for n in "gate1 g_row b_row scale2 shift2".split())
        router_w = sb("router_w", [P, KT, G + E])
        ident = sb("ident3", [P, P])
        half_neg = sb("half_neg3", [P, 1])
        eps = sb("eps3", [P, 1])
        mx = [sb(f"mx{i}", [P, H, P]) for i in range(2)]
        mx_hi = [sb(f"mx_hi{i}", [P, H, P], F32R) for i in range(2)]
        mx_lo = [sb(f"mx_lo{i}", [P, H, P], F32R) for i in range(2)]
        xt = [sb(f"xt{i}", [P, D]) for i in range(2)]
        res = [sb(f"res{i}", [P, D]) for i in range(2)]
        nrm = [sb(f"nrm{i}", [P, D]) for i in range(2)]
        x1 = [sb(f"x1_{i}", [P, D]) for i in range(2)]
        hft = [sb(f"hf_{i}", [P, D]) for i in range(2)]
        hf_t = sb("hf_t", [P, D])
        stats = sb("stats", [P, 2, 6])
        mean_var = [sb(f"mean_var{i}", [P, 2]) for i in range(2)]
        rstd = [sb(f"rstd{i}", [P, 1]) for i in range(2)]
        lg = sb("lg", [P, NT, G + E])
        py = [ps(f"py{i}", [P, 2, QW]) for i in range(2)]
        pt = ps("pt", [P, 2, QW])
        pl = ps("pl", [P, QW])

        consts, passed, rows_loaded, rows_fixed, router_loaded, logits_stored = (
            sem(n) for n in "consts3 passed3 rows_loaded rows_fixed router_loaded logits_stored".split())
        wo_loaded = [sem("wo_loaded0"), sem("wo_loaded1")]
        wo_hi_done, wo_lo_done = sem("wo_hi_done"), sem("wo_lo_done")
        mx_loaded, x_loaded, x1_stored, hf_stored = ([sem(f"{n}{i}") for i in range(2)] for n in (
            "mx_loaded", "x_loaded3_", "x1_stored", "hf_stored"))
        names = ("mx_hi_done mx_lo_done y_done gated summed stat_done aggr_done "
                 "var_eps rstd_done normed x1_g x1_done hf_s hf_done tr_done tr_taken logit_done logit_saved")
        primed = [sem(n) for n in names.split()]
        (mx_hi_done, mx_lo_done, y_done, gated, summed, stat_done, aggr_done,
         var_eps, rstd_done, normed, x1_g, x1_done, hf_s, hf_done, tr_done, tr_taken, logit_done, logit_saved) = primed
        x_v, xs_v, hf_v = (a.rearrange("(q t p) d -> q t p d", p=P, t=QT) for a in (x, x_scaled, hf))
        mixed_v = mixed.rearrange("(q h) p w -> q p h w", h=H)
        block = ctx.enter_context(nc.Block())

        def through(t):
            return t + 1 + PRIME

        def loaded(t, par):
            return 8 * (t - par) + 16

        def stored(t, par):
            return 8 * (t - par) + 32

        def all_tiles(eng, tile):
            with eng.Fori(0, NT // 2 - 2) as pair:
                for par in range(2):
                    tile(pair * 2 + par, par, 3)
            for left in range(3, -1, -1):
                tile(NT - 1 - left, (NT - 1 - left) % 2, left)

        @block.sync
        def _(sp):
            for s in primed:
                sp.sem_inc(s, PRIME)
            for s in (*x1_stored, *hf_stored):
                sp.sem_inc(s, 16)

            def load(q, j):
                t, par = q * QT + j, j % 2
                sp.wait_ge(mx_lo_done, through(t - 2))
                sp.dma_start(mx[par][:].rearrange("p h (a n) -> p a h n", a=1),
                             mixed_v[bass.ds(q, 1), :, :, j * P:(j + 1) * P].rearrange("a p h n -> p a h n")).then_inc(mx_loaded[par], 16)
                sp.wait_ge(summed, through(t - 2))
                sp.dma_start(xt[par][:].rearrange("p (a n) -> p a n", a=1), x_v[bass.ds(q, 1), j].rearrange("a p n -> p a n")).then_inc(x_loaded[par], 16)

            def store(q, j):
                t, par = q * QT + j, j % 2
                sp.wait_ge(x1_done, through(t))
                sp.dma_start(xs_v[bass.ds(q, 1), j].rearrange("a p n -> p a n"), x1[par][:].rearrange("p (a n) -> p a n", a=1)).then_inc(x1_stored[par], 16)
                sp.wait_ge(hf_done, through(t))
                sp.dma_start(hf_v[bass.ds(q, 1), j].rearrange("a p n -> p a n"), hft[par][:].rearrange("p (a n) -> p a n", a=1)).then_inc(hf_stored[par], 16)

            for h in range(2):
                sp.dma_start(wo_raw[h][:], w_out[h * P:(h + 1) * P, :]).then_inc(wo_loaded[h], 16)
            load(0, 0)
            for h in range(2, H):
                sp.wait_ge(wo_lo_done, h - 1)
                sp.dma_start(wo_raw[h % 2][:], w_out[h * P:(h + 1) * P, :]).then_inc(wo_loaded[h % 2], 16)
                if h == 3:
                    for row, src in ((gate1, mod_rows[0:1, 2 * D:3 * D]), (g_row, ln1_g), (b_row, ln1_b),
                                     (scale2, mod_rows[0:1, 4 * D:5 * D]), (shift2, mod_rows[0:1, 3 * D:4 * D])):
                        sp.dma_start(row[:], src.to_broadcast([P, D])).then_inc(rows_loaded, 16)
            sp.dma_start(router_w[:, :, 0:G], w_grp.rearrange("(k p) n -> p k n", p=P)).then_inc(router_loaded, 16)
            sp.dma_start(router_w[:, :, G:], w_exp.rearrange("(k p) n -> p k n", p=P)).then_inc(router_loaded, 16)
            load(0, 1)

            load(0, 2)
            load(0, 3)
            store(0, 0)
            with sp.Fori(1, NQ) as q:
                for j in range(QT):
                    load(q, j)
                    store(*((q, j - 3) if j >= 3 else (q - 1, j + 1)))
            store(NQ - 1, 1)
            store(NQ - 1, 2)
            store(NQ - 1, 3)
            sp.wait_ge(logit_saved, through(NT - 1))
            sp.dma_start(logits, lg[:].rearrange("p t n -> p (t n)")).then_inc(logits_stored, 16)
            sp.wait_ge(logits_stored, 16)
            for par in range(2):
                sp.wait_ge(x1_stored[par], stored(NT - 2 + par, par))
                sp.wait_ge(hf_stored[par], stored(NT - 2 + par, par))

        @block.gpsimd
        def _(pool):
            nc.gpsimd.memset(ident[:], 0.0).then_inc(consts, 1)
            nc.gpsimd.memset(half_neg[:], -0.5).then_inc(consts, 1)
            nc.gpsimd.memset(eps[:], 1e-5).then_inc(consts, 1)
            pool.wait_ge(consts, 3)
            nc.gpsimd.affine_select(out=ident[:], in_=ident[:], compare_op=ALU.not_equal, fill=1.0, base=0,
                                    pattern=[[-1, P]], channel_multiplier=1).then_inc(consts, 1)
            for h in range(H):
                pool.wait_ge(wo_hi_done, h + 1)
                pool.wait_ge(wo_loaded[h % 2], 16 * (h // 2 + 1))
                nc.gpsimd.tensor_tensor(wo_lo[:, h, :], wo_raw[h % 2][:], wo_hi[:, h, :].bitcast(F32), ALU.subtract).then_inc(wo_lo_done, 1)
            pool.wait_ge(rows_loaded, 16 * 5)
            nc.gpsimd.tensor_tensor(nrm[1][:], b_row[:], scale2[:], ALU.mult).then_inc(rows_fixed, 1)
            pool.wait_ge(rows_fixed, 1)
            nc.gpsimd.tensor_tensor(shift2[:], shift2[:], nrm[1][:], ALU.add).then_inc(rows_fixed, 1)
            nc.gpsimd.tensor_tensor(scale2[:], scale2[:], g_row[:], ALU.mult).then_inc(rows_fixed, 1)
            pool.wait_ge(rows_fixed, 3)
            nc.gpsimd.tensor_scalar(g_row[:], g_row[:], ALPHA, 1.0, ALU.mult, ALU.mult).then_inc(rows_fixed, 1)
            nc.gpsimd.tensor_scalar(b_row[:], b_row[:], ALPHA, 1.0, ALU.mult, ALU.mult).then_inc(rows_fixed, 1)

            def tile(t, par, left):
                V = through(t)
                pool.wait_ge(aggr_done, V)
                pool.wait_ge(normed, V - 2)
                nc.gpsimd.tensor_tensor(rstd[par][:], mean_var[par][:, 1:2], eps[:], ALU.add).then_inc(var_eps, 1)
                pool.wait_ge(var_eps, V)
                nc.gpsimd.tensor_tensor(rstd[par][:], rstd[par][:], half_neg[:], ALU.pow).then_inc(rstd_done, 1)
                pool.wait_ge(normed, V)
                pool.wait_ge(hf_stored[par], stored(t - 2, par))
                pool.wait_ge(tr_done, V - 2)
                nc.gpsimd.tensor_tensor(hft[par][:], nrm[par][:], scale2[:], ALU.mult).then_inc(hf_s, 1)
                pool.wait_ge(hf_s, V)
                nc.gpsimd.tensor_tensor(hft[par][:], hft[par][:], shift2[:], ALU.add).then_inc(hf_done, 1)

            all_tiles(pool, tile)

        @block.scalar
        def _(act):
            for h in range(H):
                act.wait_ge(wo_loaded[h % 2], 16 * (h // 2 + 1))
                nc.scalar.copy(wo_hi[:, h, :], wo_raw[h % 2][:]).then_inc(wo_hi_done, 1)

            def split_high(t, par):
                act.wait_ge(mx_loaded[par], loaded(t, par))
                act.wait_ge(y_done, through(t - 2))
                nc.scalar.copy(mx_hi[par][:], mx[par][:]).then_inc(mx_hi_done, 1)

            split_high(0, 0)
            split_high(1, 1)
            split_high(2, 0)

            def tile(t, par, left):
                V = through(t)
                if left >= 3:
                    split_high(t + 3, 1 - par)
                act.wait_ge(tr_done, V)
                act.wait_ge(logit_done, V - 1)
                nc.scalar.copy(hf_t[:].rearrange("p (b n) -> p b n", b=2), pt[:]).then_inc(tr_taken, 1)
                act.wait_ge(logit_done, V)
                nc.scalar.copy(lg[:, bass.ds(t, 1), :].rearrange("p a n -> p (a n)"), pl[:, 0:G + E]).then_inc(logit_saved, 1)

            all_tiles(act, tile)

        @block.vector
        def _(dve):
            def split_low(t, par):
                dve.wait_ge(mx_loaded[par], loaded(t, par))
                dve.wait_ge(mx_hi_done, through(t))
                dve.wait_ge(y_done, through(t - 2))
                nc.vector.tensor_tensor(mx_lo[par][:], mx[par][:], mx_hi[par][:].bitcast(F32), ALU.subtract).then_inc(mx_lo_done, 1)

            split_low(0, 0)
            split_low(1, 1)
            dve.wait_ge(rows_loaded, 16 * 5)
            dve.wait_ge(rows_fixed, 5)

            def tile(t, par, left):
                V = through(t)
                if left >= 2:
                    split_low(t + 2, par)
                halves = lambda a: a[:].rearrange("p (b n) -> p b n", b=2)
                dve.wait_ge(y_done, V)
                dve.wait_ge(normed, V - 2)
                nc.vector.tensor_tensor(halves(res[par]), py[par][:], halves(gate1), ALU.mult).then_inc(gated, 1)
                dve.wait_ge(gated, V)
                dve.wait_ge(x_loaded[par], loaded(t, par))
                nc.vector.scalar_tensor_tensor(res[par][:], xt[par][:], ALPHA, res[par][:], ALU.mult, ALU.add).then_inc(summed, 1)
                dve.wait_ge(summed, V)
                dve.wait_ge(aggr_done, V - 1)
                for b in range(2):
                    nc.vector.bn_stats(stats[:, b, :], res[par][:, b * QW:(b + 1) * QW]).then_inc(stat_done, 1)
                dve.wait_ge(normed, V - 2)
                dve.wait_ge(stat_done, 2 * (t + 1) + PRIME)
                dve.sem_inc(passed, 1)
                nc.vector.bn_aggr(mean_var[par][:], stats[:]).then_inc(aggr_done, 1)
                dve.wait_ge(rstd_done, V)
                dve.wait_ge(hf_s, V - 2)
                dve.wait_ge(x1_g, V - 2)
                nc.vector.tensor_scalar(nrm[par][:], res[par][:], mean_var[par][:, 0:1], rstd[par][:], ALU.subtract, ALU.mult).then_inc(normed, 1)
                dve.wait_ge(normed, V)
                dve.wait_ge(x1_stored[par], stored(t - 2, par))
                nc.vector.tensor_tensor(x1[par][:], nrm[par][:], g_row[:], ALU.mult).then_inc(x1_g, 1)
                dve.wait_ge(x1_g, V)
                nc.vector.tensor_tensor(x1[par][:], x1[par][:], b_row[:], ALU.add).then_inc(x1_done, 1)

            all_tiles(dve, tile)

        @block.tensor
        def _(pe):
            pe.wait_ge(wo_hi_done, H)
            pe.wait_ge(wo_lo_done, H)

            def project(t, par):
                pe.wait_ge(mx_hi_done, through(t))
                pe.wait_ge(mx_lo_done, through(t))
                pe.wait_ge(gated, through(t - 2))
                for h in range(H):
                    for s, (a, w) in enumerate(((mx_hi, wo_hi), (mx_hi, wo_lo), (mx_lo, wo_hi))):
                        for n in range(2):
                            last = nc.tensor.matmul(py[par][:, n, :], a[par][:, h, :], w[:, h, n * QW:(n + 1) * QW],
                                                    start=(h == 0 and s == 0), stop=(h == H - 1 and s == 2))
                last.then_inc(y_done, 1)

            project(0, 0)
            project(1, 1)
            pe.wait_ge(consts, 4)
            pe.wait_ge(router_loaded, 32)

            def tile(t, par, left):
                V = through(t)
                if left >= 2:
                    project(t + 2, par)
                pe.wait_ge(hf_done, V)
                pe.wait_ge(tr_taken, V - 1)
                for k in range(KT):
                    last = nc.tensor.transpose(pt[:, k // QT, (k % QT) * P:(k % QT + 1) * P], hft[par][:, k * P:(k + 1) * P], ident[:])
                last.then_inc(tr_done, 1)
                pe.wait_ge(tr_taken, V)
                pe.wait_ge(logit_saved, V - 1)
                for k in range(KT):
                    last = nc.tensor.matmul(pl[:, 0:G + E], hf_t[:, k * P:(k + 1) * P], router_w[:, k, :], start=(k == 0), stop=(k == KT - 1))
                last.then_inc(logit_done, 1)

            all_tiles(pe, tile)


NBLK = 64
NA = 2 * NT


def routing_phase(nc, logits, b_grp, b_exp, slot_token, choice_row, choice_gate, block_ends):
    with ExitStack() as ctx:
        sb, ps, sem = allocators(nc, ctx, "route")
        lg = sb("lg4", [P, NT, G + E])
        bias = sb("bias4", [P, G + E])
        prefer = sb("prefer", [P, EPG])
        iota_i = sb("iota_i", [P, P], I32)
        lane = sb("lane", [P, P])
        tok_i = sb("tok_i", [P, NT], I32)
        token = sb("token", [P, NT])
        steps128 = sb("steps128", [P, NBLK])
        strict = sb("strict", [P, P])
        ones = sb("ones4", [P, P])
        g_top, g_sum, g_prob, v_top, m1, m2, ed, den = (
            sb(n, [P, NT]) for n in "g_top g_sum g_prob v_top m1 m2 ed den".split())
        g_val = sb("g_val", [P, NT, G])
        g_exp = sb("g_exp", [P, NT, G])
        g_hot = sb("g_hot", [P, NT, G])
        picked = sb("picked", [P, NT, G, EPG])
        el = sb("el", [P, NT, EPG])
        el2 = sb("el2", [P, NT, EPG])
        e_val = sb("e_val", [P, NT, EPG])
        e_hot = [sb(f"e_hot{i}", [P, NT, EPG]) for i in range(2)]
        hot = sb("hot", [P, 2, NT, G, EPG])
        hot_sum = sb("hot_sum", [P, NT, E])
        totals = sb("totals", [P, NT, E])
        carry = sb("carry", [P, NT, E])
        rank = sb("rank", [P, NT, E])
        count = sb("count", [P, E])
        over = sb("over", [P, E, NT])
        ends = [sb(f"ends{i}", [P, E]) for i in range(2)]
        blocks = sb("blocks", [P, E])
        base = sb("base", [P, E])
        weighted = sb("weighted", [P, 2, NT, E])
        slot = sb("slot", [P, NA])
        past = sb("past", [P, NA, NBLK])
        blk = sb("blk", [P, NA])
        off = sb("off", [P, NA])
        off_hot = sb("off_hot", [P, NA, P])
        blk_tok = sb("blk_tok", [P, NA, NBLK])
        gates = sb("gates", [P, 2, NT])
        rows_i = sb("rows_i", [P, NA], I32)
        slots_i = sb("slots_i", [P, NBLK], I32)
        ends_i = sb("ends_i", [1, E + 2], I32)
        p_cum = ps("p_cum4", [P, QW])
        p_tot = ps("p_tot4", [P, QW])
        p_slot = ps("p_slot", [P, QW])

        loaded, consts, const_f, group_ready, group_exp, gap_ready, gap_exp, hot_ready, counted, slots_ready, placed, step, stored = (
            sem(n) for n in "loaded4 consts4 const_f group_ready group_exp gap_ready gap_exp hot_ready counted slots_ready placed step4 stored4".split())
        block = ctx.enter_context(nc.Block())

        @block.sync
        def _(sp):
            sp.dma_start(lg[:].rearrange("p t n -> p (t n)"), logits).then_inc(loaded, 16)
            sp.dma_start(bias[:, 0:G], b_grp.to_broadcast([P, G])).then_inc(loaded, 16)
            sp.dma_start(bias[:, G:], b_exp.to_broadcast([P, E])).then_inc(loaded, 16)
            sp.wait_ge(stored, 1)
            sp.dma_start(choice_row, rows_i[:]).then_inc(stored, 16)
            sp.dma_start(choice_gate, gates[:].rearrange("p c t -> p (c t)")).then_inc(stored, 16)
            sp.dma_start(slot_token, slots_i[:]).then_inc(stored, 16)
            sp.dma_start(block_ends, ends_i[:]).then_inc(stored, 16)
            sp.wait_ge(stored, 65)

        @block.gpsimd
        def _(pool):
            nc.gpsimd.memset(ones[:], 1.0).then_inc(consts, 1)
            nc.gpsimd.memset(strict[:], 1.0).then_inc(consts, 1)
            nc.gpsimd.iota(iota_i[:], pattern=[[1, P]], base=0, channel_multiplier=0).then_inc(consts, 1)
            nc.gpsimd.iota(tok_i[:], pattern=[[P, NT]], base=0, channel_multiplier=1).then_inc(consts, 1)
            pool.wait_ge(consts, 4)
            nc.gpsimd.affine_select(out=strict[:], in_=strict[:], compare_op=ALU.is_ge, fill=0.0, base=-1,
                                    pattern=[[1, P]], channel_multiplier=-1).then_inc(consts, 1)

        @block.tensor
        def _(pe):
            pe.wait_ge(consts, 5)
            pe.wait_ge(hot_ready, 1)
            h = hot_sum[:].rearrange("p t e -> p (t e)")
            nc.tensor.matmul(p_cum[:], strict[:], h, start=True, stop=True).then_inc(counted, 1)
            nc.tensor.matmul(p_tot[:], ones[:], h, start=True, stop=True).then_inc(counted, 1)
            pe.wait_ge(slots_ready, 2)
            for a in range(NA):
                last = nc.tensor.matmul(p_slot[:, 0:NBLK], off_hot[:, a, :], blk_tok[:, a, :], start=(a == 0), stop=(a == NA - 1))
            last.then_inc(placed, 1)

        @block.scalar
        def _(act):
            act.wait_ge(group_ready, 1)
            nc.scalar.activation(g_exp[:], g_val[:], ACT.Exp).then_inc(group_exp, 1)
            act.wait_ge(gap_ready, 1)
            nc.scalar.activation(ed[:], m2[:], ACT.Exp).then_inc(gap_exp, 1)

        @block.vector
        def _(dve):
            dve.wait_ge(consts, 4)
            nc.vector.tensor_copy(lane[:], iota_i[:]).then_inc(const_f, 1)
            nc.vector.tensor_copy(token[:], tok_i[:]).then_inc(const_f, 1)
            dve.wait_ge(const_f, 2)
            nc.vector.tensor_scalar(steps128[:], lane[:, 0:NBLK], float(P), float(P), ALU.mult, ALU.add).then_inc(const_f, 1)
            nc.vector.tensor_scalar(prefer[:], lane[:, 0:EPG], -1.0, float(EPG), ALU.mult, ALU.add).then_inc(const_f, 1)
            dve.wait_ge(const_f, 4)

            dve.wait_ge(loaded, 48)
            nc.vector.tensor_tensor(lg[:], lg[:], bias[:].unsqueeze(1).to_broadcast([P, NT, G + E]), ALU.add).then_inc(step, 1)
            n = 1
            dve.wait_ge(step, n)
            nc.vector.tensor_reduce(g_top[:], lg[:, :, 0:G], AX.X, ALU.max).then_inc(step, 1)
            n += 1
            dve.wait_ge(step, n)
            nc.vector.tensor_tensor(g_val[:], lg[:, :, 0:G], g_top[:].unsqueeze(2).to_broadcast([P, NT, G]), ALU.subtract).then_inc(group_ready, 1)
            dve.wait_ge(group_exp, 1)
            nc.vector.tensor_reduce(g_sum[:], g_exp[:], AX.X, ALU.add).then_inc(step, 1)
            n += 1
            dve.wait_ge(step, n)
            nc.vector.reciprocal(g_prob[:], g_sum[:]).then_inc(step, 1)
            n += 1
            dve.wait_ge(step, n)
            nc.vector.tensor_scalar(g_hot[:], g_val[:], 0.0, None, ALU.is_ge).then_inc(step, 1)
            n += 1

            def first_hot(out, eq, top, width, n):
                dve.wait_ge(step, n)
                nc.vector.tensor_tensor(eq[:], eq[:], prefer[:, EPG - width:].unsqueeze(1).to_broadcast([P, NT, width]), ALU.mult).then_inc(step, 1)
                dve.wait_ge(step, n + 1)
                nc.vector.tensor_reduce(top[:], eq[:], AX.X, ALU.max).then_inc(step, 1)
                dve.wait_ge(step, n + 2)
                nc.vector.tensor_tensor(out[:], eq[:], top[:].unsqueeze(2).to_broadcast([P, NT, width]), ALU.is_equal).then_inc(step, 1)
                return n + 3

            n = first_hot(g_hot, g_hot, v_top, G, n)
            dve.wait_ge(step, n)
            nc.vector.tensor_tensor(picked[:], lg[:, :, G:].rearrange("p t (g e) -> p t g e", g=G),
                                    g_hot[:].unsqueeze(3).to_broadcast([P, NT, G, EPG]), ALU.mult).then_inc(step, 1)
            n += 1
            dve.wait_ge(step, n)
            nc.vector.tensor_reduce(el[:], picked[:].rearrange("p t g e -> p t e g"), AX.X, ALU.add).then_inc(step, 1)
            n += 1
            for c, (src, m) in enumerate(((el, m1), (el2, m2))):
                dve.wait_ge(step, n)
                nc.vector.tensor_reduce(m[:], src[:], AX.X, ALU.max).then_inc(step, 1)
                n += 1
                dve.wait_ge(step, n)
                nc.vector.tensor_tensor(e_val[:], src[:], m[:].unsqueeze(2).to_broadcast([P, NT, EPG]), ALU.is_equal).then_inc(step, 1)
                n += 1
                n = first_hot(e_hot[c], e_val, v_top, EPG, n)
                if c == 0:
                    dve.wait_ge(step, n)
                    nc.vector.scalar_tensor_tensor(el2[:], e_hot[0][:], -1e30, el[:], ALU.mult, ALU.add).then_inc(step, 1)
                    n += 1
            dve.wait_ge(step, n)
            nc.vector.tensor_tensor(m2[:], m2[:], m1[:], ALU.subtract).then_inc(gap_ready, 1)
            for c in range(2):
                nc.vector.tensor_tensor(hot[:, c], g_hot[:].unsqueeze(3).to_broadcast([P, NT, G, EPG]),
                                        e_hot[c][:].unsqueeze(2).to_broadcast([P, NT, G, EPG]), ALU.mult).then_inc(step, 1)
                n += 1
            hots = hot[:].rearrange("p c t g e -> p c t (g e)")
            dve.wait_ge(step, n)
            nc.vector.tensor_tensor(hot_sum[:], hots[:, 0], hots[:, 1], ALU.add).then_inc(hot_ready, 1)
            dve.wait_ge(gap_exp, 1)
            nc.vector.tensor_scalar(den[:], ed[:], 1.0, None, ALU.add).then_inc(step, 1)
            n += 1
            dve.wait_ge(step, n)
            nc.vector.reciprocal(den[:], den[:]).then_inc(step, 1)
            n += 1
            dve.wait_ge(step, n)
            nc.vector.tensor_tensor(gates[:, 0], den[:], g_prob[:], ALU.mult).then_inc(step, 1)
            n += 1
            dve.wait_ge(step, n)
            nc.vector.tensor_tensor(gates[:, 1], gates[:, 0], ed[:], ALU.mult).then_inc(step, 1)
            n += 1
            dve.wait_ge(counted, 2)
            nc.vector.tensor_copy(totals[:].rearrange("p t e -> p (t e)"), p_tot[:]).then_inc(step, 1)
            nc.vector.memset(carry[:, 0], 0.0).then_inc(step, 1)
            n += 2
            for t in range(1, NT):
                dve.wait_ge(step, n)
                nc.vector.tensor_tensor(carry[:, t], carry[:, t - 1], totals[:, t - 1], ALU.add).then_inc(step, 1)
                n += 1
            dve.wait_ge(step, n)
            nc.vector.tensor_tensor(rank[:].rearrange("p t e -> p (t e)"), carry[:].rearrange("p t e -> p (t e)"), p_cum[:], ALU.add).then_inc(step, 1)
            nc.vector.tensor_tensor(count[:], carry[:, NT - 1], totals[:, NT - 1], ALU.add).then_inc(step, 1)
            n += 2
            dve.wait_ge(step, n)
            nc.vector.tensor_tensor(over[:], count[:].unsqueeze(2).to_broadcast([P, E, NT]),
                                    steps128[:, 0:NT].unsqueeze(1).to_broadcast([P, E, NT]), ALU.is_gt).then_inc(step, 1)
            n += 1
            dve.wait_ge(step, n)
            nc.vector.tensor_reduce(blocks[:], over[:], AX.X, ALU.add).then_inc(step, 1)
            n += 1
            dve.wait_ge(step, n)
            nc.vector.tensor_scalar(ends[0][:], blocks[:], 1.0, None, ALU.add).then_inc(step, 1)
            n += 1
            dve.wait_ge(step, n)
            nc.vector.tensor_copy(blocks[:], ends[0][:]).then_inc(step, 1)
            n += 1
            for r in range(5):
                s, a, b = 1 << r, ends[r % 2], ends[1 - r % 2]
                dve.wait_ge(step, n)
                nc.vector.tensor_copy(b[:, 0:s], a[:, 0:s]).then_inc(step, 1)
                nc.vector.tensor_tensor(b[:, s:], a[:, s:], a[:, 0:E - s], ALU.add).then_inc(step, 1)
                n += 2
            end = ends[1]
            dve.wait_ge(step, n)
            nc.vector.tensor_tensor(base[:], end[:], blocks[:], ALU.subtract).then_inc(step, 1)
            nc.vector.memset(ends_i[:, 0:2], 0).then_inc(step, 1)
            nc.vector.tensor_copy(ends_i[:, 2:], end[0:1, :]).then_inc(step, 1)
            n += 3
            dve.wait_ge(step, n)
            nc.vector.tensor_scalar(base[:], base[:], float(P), None, ALU.mult).then_inc(step, 1)
            n += 1
            dve.wait_ge(step, n)
            nc.vector.tensor_tensor(rank[:], rank[:], base[:].unsqueeze(1).to_broadcast([P, NT, E]), ALU.add).then_inc(step, 1)
            n += 1
            dve.wait_ge(step, n)
            nc.vector.tensor_tensor(weighted[:], hots, rank[:].unsqueeze(1).to_broadcast([P, 2, NT, E]), ALU.mult).then_inc(step, 1)
            n += 1
            dve.wait_ge(step, n)
            nc.vector.tensor_reduce(slot[:].rearrange("p (c t) -> p c t", c=2), weighted[:], AX.X, ALU.add).then_inc(step, 1)
            n += 1
            dve.wait_ge(step, n)
            nc.vector.tensor_scalar(rows_i[:], slot[:], float(P), None, ALU.add).then_inc(step, 1)
            nc.vector.tensor_tensor(past[:], slot[:].unsqueeze(2).to_broadcast([P, NA, NBLK]),
                                    steps128[:].unsqueeze(1).to_broadcast([P, NA, NBLK]), ALU.is_ge).then_inc(step, 1)
            n += 2
            dve.wait_ge(step, n)
            nc.vector.tensor_reduce(blk[:], past[:], AX.X, ALU.add).then_inc(step, 1)
            n += 1
            dve.wait_ge(step, n)
            nc.vector.scalar_tensor_tensor(off[:], blk[:], -float(P), slot[:], ALU.mult, ALU.add).then_inc(step, 1)
            nc.vector.tensor_tensor(blk_tok[:], blk[:].unsqueeze(2).to_broadcast([P, NA, NBLK]),
                                    lane[:, 0:NBLK].unsqueeze(1).to_broadcast([P, NA, NBLK]), ALU.is_equal).then_inc(step, 1)
            n += 2
            dve.wait_ge(step, n)
            nc.vector.tensor_tensor(off_hot[:], off[:].unsqueeze(2).to_broadcast([P, NA, P]),
                                    lane[:].unsqueeze(1).to_broadcast([P, NA, P]), ALU.is_equal).then_inc(slots_ready, 1)
            b4 = blk_tok[:].rearrange("p (c t) b -> p c t b", c=2)
            nc.vector.tensor_tensor(b4, b4, token[:].unsqueeze(1).unsqueeze(3).to_broadcast([P, 2, NT, NBLK]), ALU.mult).then_inc(slots_ready, 1)
            dve.wait_ge(placed, 1)
            nc.vector.tensor_copy(slots_i[:], p_slot[:, 0:NBLK]).then_inc(step, 1)
            n += 1
            dve.wait_ge(step, n)
            nc.vector.memset(den[:, 0:1], 0.0).then_inc(stored, 1)


RING = 16
SLABS = KT + FT
PAIRS = SLABS // 2
UP_KT = KT // 2
AHEAD = RING - SLABS
UNROLL = 4
POOL_PAIRS = (1, 4)
QUARTER = DE // 2
YROWS = (NBLK + 1) * P


def expert_phase(nc, hf, slot_token, block_ends, mod_rows, w_gate, w_up, w_down, y_rows):
    with ExitStack() as ctx:
        sb, ps, sem = allocators(nc, ctx, "expert")
        raw = [sb(f"raw{i}", [P, 2, D]) for i in range(PAIRS)]
        w_hi = sb("w_hi5", [P, RING, D], F32R)
        w_lo = sb("w_lo5", [P, RING, D], F32R)
        x_tok = sb("x_tok5", [P, D])
        x_hi = sb("x_hi", [P, KT, P], F32R)
        x_lo = sb("x_lo", [P, KT, P], F32R)
        gate_s = sb("gate_s", [P, 2, QUARTER])
        hid = sb("hid", [P, DE])
        hid_hi = sb("hid_hi", [P, FT, P], F32R)
        hid_lo = sb("hid_lo", [P, FT, P], F32R)
        y_out = sb("y_out", [P, D])
        gate2 = sb("gate2", [P, D])
        ident = sb("ident5", [P, P])
        table = sb("table", [P, NBLK + 1], I32)
        ends = sb("ends5", [1, E + 2], I32)
        zeros = sb("zeros", [P, DE])
        index = sb("index5", [P, 1], I32)
        p_gate = ps("p_gate", [P, DE])
        p_up = ps("p_up", [P, DE])
        p_x = [ps(f"p_x{i}", [P, QW]) for i in range(2)]
        p_hid = [ps(f"p_hid{i}", [P, QW]) for i in range(2)]
        p_y = ps("p_y", [P, D])

        consts, passed, zeros_stored, y_cleared, table_loaded, ends_loaded, gate2_loaded = (
            sem(n) for n in "consts5 passed5 zeros_stored y_cleared table_loaded ends_loaded gate2_loaded".split())
        w_loaded = [sem(f"w_loaded5_{i}") for i in range(PAIRS)]
        hi_made = [sem(f"hi_made{i}") for i in range(PAIRS)]
        lo_made = [sem(f"lo_made{i}") for i in range(PAIRS)]
        two = lambda name: [sem(f"{name}{i}") for i in range(2)]
        x_tr, x_hi_done, x_lo_done = two("x_tr"), two("x_hi_done"), two("x_lo_done")
        silu_done, hid_done, hid_tr, hid_hi_done, hid_lo_done = (
            two("silu_done"), two("hid_done"), two("hid_tr"), two("hid_hi_done"), two("hid_lo_done"))
        index_copied, gathered, up_done, down_done, y_scaled, y_stored = (
            sem(n) for n in "index_copied gathered up_done down_done y_scaled y_stored".split())
        primed = [*hi_made, *lo_made, *x_tr, *x_hi_done, *x_lo_done, *silu_done, *hid_done, *hid_tr, *hid_hi_done,
                  *hid_lo_done, index_copied, up_done, down_done, y_scaled]
        up_v = [w.rearrange("(a u) (k p) n -> a u p k n", u=UNROLL, p=P) for w in (w_gate, w_up)]
        down_v = w_down.rearrange("(a u) (k p) n -> a u p k n", u=UNROLL, p=P)
        block = ctx.enter_context(nc.Block())

        def through(b):
            return b + 1 + PRIME

        def scaled(b):
            return b + 2 + PRIME

        def made(e):
            return 2 * e + 2 + PRIME

        def slot(u, k):
            return (SLABS * u + k) % RING

        def bounds(eng, e):
            first = eng.value_load(ends[0:1, bass.ds(e + 1, 1)], min_val=0, max_val=NBLK - 1)
            end = eng.value_load(ends[0:1, bass.ds(e + 2, 1)], min_val=1, max_val=NBLK - 1)
            return first, end

        def all_experts(eng, expert):
            with eng.Fori(0, E // UNROLL - 1) as a:
                for u in range(UNROLL):
                    expert(a * UNROLL + u, u, True)
            for u in range(UNROLL):
                expert(E - UNROLL + u, u, u < UNROLL - 1)

        def splits(eng, pairs, split):
            def ahead(e, u, first):
                eng.wait_ge(down_done, first + PRIME)
                for i in pairs:
                    if 2 * i < AHEAD:
                        split(e, u, i)

            def behind(e, u, end):
                eng.wait_ge(up_done, end + PRIME)
                for i in pairs:
                    if 2 * i >= AHEAD:
                        split(e, u, i)
            return ahead, behind

        def loaded(e, i):
            return (32 if i < UP_KT else 16) * (e + 1)

        @block.sync
        def _(sp):
            for s in primed:
                sp.sem_inc(s, PRIME)
            sp.sem_inc(y_stored, 16)
            sp.dma_start(ends[:], block_ends).then_inc(ends_loaded, 16)
            sp.dma_start(table[:, 0:NBLK], slot_token).then_inc(table_loaded, 16)
            sp.dma_start(gate2[:], mod_rows[0:1, 5 * D:].to_broadcast([P, D])).then_inc(gate2_loaded, 16)
            with sp.Fori(0, E // UNROLL) as a:
                for u in range(UNROLL):
                    for i in range(PAIRS):
                        sp.wait_ge(hi_made[i], 2 * (a * UNROLL + u) + PRIME)
                        sp.wait_ge(lo_made[i], 2 * (a * UNROLL + u) + PRIME)
                        if i < UP_KT:
                            for s in range(2):
                                sp.dma_start(raw[i][:, :, s * DE:(s + 1) * DE].rearrange("p (a k) n -> p a k n", a=1),
                                             up_v[s][bass.ds(a, 1), u, :, 2 * i:2 * i + 2, :].rearrange("a p k n -> p a k n")
                                             ).then_inc(w_loaded[i], 16)
                        else:
                            k = 2 * (i - UP_KT)
                            sp.dma_start(raw[i][:].rearrange("p (a k) n -> p a k n", a=1),
                                         down_v[bass.ds(a, 1), u, :, k:k + 2, :].rearrange("a p k n -> p a k n")
                                         ).then_inc(w_loaded[i], 16)
            sp.wait_ge(consts, 3)
            sp.wait_ge(ends_loaded, 16)
            last = sp.value_load(ends[0:1, E + 1:E + 2], min_val=1, max_val=NBLK - 1)
            with sp.Fori(last + 1, NBLK + 1) as b:
                sp.dma_start(y_rows[bass.ds(b * P, P), :].rearrange("p (r n) -> p r n", n=DE),
                             zeros[:].unsqueeze(1).to_broadcast([P, D // DE, DE])).then_inc(zeros_stored, 16)
            with sp.Fori(0, last + 1):
                sp.sem_inc(zeros_stored, 16)
            sp.wait_ge(zeros_stored, 16 * (NBLK + 1))

        @block.gpsimd
        def _(pool):
            nc.gpsimd.memset(ident[:], 0.0).then_inc(consts, 1)
            nc.gpsimd.memset(zeros[:], 0.0).then_inc(consts, 1)
            pool.wait_ge(consts, 2)
            nc.gpsimd.affine_select(out=ident[:], in_=ident[:], compare_op=ALU.not_equal, fill=1.0, base=0,
                                    pattern=[[-1, P]], channel_multiplier=1).then_inc(consts, 1)

            def gather(b):
                nc.gpsimd.tensor_copy(index[:], table[:, bass.ds(b, 1)]).then_inc(index_copied, 1)
                pool.wait_ge(index_copied, through(b))
                pool.sem_inc(passed, 1)
                nc.gpsimd.indirect_dma_start(x_tok[:], None, hf, bass.IndirectOffsetOnAxis(ap=index[:].bitcast(U32), axis=0)).then_inc(gathered, 16)

            def split(e, u, i):
                pool.wait_ge(w_loaded[i], loaded(e, i))
                pool.wait_ge(hi_made[i], made(e))
                for j in range(2):
                    k = slot(u, 2 * i + j)
                    nc.gpsimd.tensor_tensor(w_lo[:, k, :], raw[i][:, j, :], w_hi[:, k, :].bitcast(F32), ALU.subtract).then_inc(lo_made[i], 1)

            ahead, behind = splits(pool, POOL_PAIRS, split)
            nc.gpsimd.memset(table[:, NBLK:], 0).then_inc(consts, 1)
            pool.wait_ge(consts, 4)
            pool.wait_ge(table_loaded, 16)
            gather(0)
            pool.wait_ge(gathered, 16)
            pool.wait_ge(x_tr[1], through(0))
            gather(1)
            pool.wait_ge(ends_loaded, 16)
            for i in POOL_PAIRS:
                split(0, 0, i)

            def expert(e, u, more):
                first, end = bounds(pool, e)
                if more:
                    ahead(e + 1, (u + 1) % UNROLL, first)
                with pool.Fori(first, end) as b:
                    pool.wait_ge(gathered, 16 * (b + 2))
                    pool.wait_ge(x_tr[1], through(b + 1))
                    gather(b + 2)
                if more:
                    behind(e + 1, (u + 1) % UNROLL, end)

            all_experts(pool, expert)
            last = pool.value_load(ends[0:1, E + 1:E + 2], min_val=1, max_val=NBLK - 1)
            pool.wait_ge(gathered, 16 * (last + 2))
            pool.wait_ge(y_stored, 16 * last + 32)

        @block.scalar
        def _(act):
            def split(e, u, i):
                act.wait_ge(w_loaded[i], loaded(e, i))
                for j in range(2):
                    nc.scalar.copy(w_hi[:, slot(u, 2 * i + j), :], raw[i][:, j, :]).then_inc(hi_made[i], 1)

            ahead, behind = splits(act, range(PAIRS), split)

            def round_x(b):
                for n in range(2):
                    act.wait_ge(x_tr[n], through(b))
                    nc.scalar.copy(x_hi[:, n * QT:(n + 1) * QT, :].rearrange("p k n -> p (k n)"), p_x[n][:]).then_inc(x_hi_done[n], 1)

            def store(b):
                act.wait_ge(y_scaled, scaled(b - 1))
                act.dma_start(y_rows[bass.ds(b * P, P), :], y_out[:]).then_inc(y_stored, 16)

            for i in range(PAIRS):
                split(0, 0, i)
                if i == 0:
                    round_x(0)
            act.wait_ge(ends_loaded, 16)

            def expert(e, u, more):
                first, end = bounds(act, e)
                if more:
                    ahead(e + 1, (u + 1) % UNROLL, first)
                with act.Fori(first, end) as b:
                    store(b)
                    act.wait_ge(up_done, through(b))
                    for n in range(2):
                        act.wait_ge(hid_done[n], through(b - 1))
                        nc.scalar.activation(gate_s[:, n, :], p_gate[:, n * QUARTER:(n + 1) * QUARTER], ACT.Silu).then_inc(silu_done[n], 1)
                    act.wait_ge(down_done, through(b - 1))
                    for n in range(2):
                        act.wait_ge(hid_tr[n], through(b))
                        nc.scalar.copy(hid_hi[:, 2 * n:2 * n + 2, :].rearrange("p k n -> p (k n)"), p_hid[n][:, 0:2 * P]).then_inc(hid_hi_done[n], 1)
                    round_x(b + 1)
                if more:
                    behind(e + 1, (u + 1) % UNROLL, end)

            all_experts(act, expert)
            last = act.value_load(ends[0:1, E + 1:E + 2], min_val=1, max_val=NBLK - 1)
            store(last)

        @block.vector
        def _(dve):
            def split(e, u, i):
                dve.wait_ge(w_loaded[i], loaded(e, i))
                for j in range(2):
                    dve.wait_ge(hi_made[i], made(e) - 1 + j)
                    k = slot(u, 2 * i + j)
                    nc.vector.tensor_tensor(w_lo[:, k, :], raw[i][:, j, :], w_hi[:, k, :].bitcast(F32), ALU.subtract).then_inc(lo_made[i], 1)

            pairs = [i for i in range(PAIRS) if i not in POOL_PAIRS]
            ahead, behind = splits(dve, pairs, split)

            def low_x(b):
                for n in range(2):
                    dve.wait_ge(x_hi_done[n], through(b))
                    cols = slice(n * QT, (n + 1) * QT)
                    nc.vector.tensor_tensor(x_lo[:, cols, :].rearrange("p k n -> p (k n)"), p_x[n][:],
                                            x_hi[:, cols, :].bitcast(F32).rearrange("p k n -> p (k n)"), ALU.subtract).then_inc(x_lo_done[n], 1)

            def scale_y(b):
                dve.wait_ge(y_stored, 16 * b + 32)
                dve.wait_ge(down_done, through(b))
                nc.vector.tensor_tensor(y_out[:], p_y[:], gate2[:], ALU.mult).then_inc(y_scaled, 1)

            nc.vector.memset(p_y[:, 0:QW], 0.0).then_inc(y_cleared, 1)
            nc.vector.memset(p_y[:, QW:], 0.0).then_inc(y_cleared, 1)
            for i in pairs:
                split(0, 0, i)
                if i == 0:
                    low_x(0)
            dve.wait_ge(y_cleared, 2)
            dve.wait_ge(gate2_loaded, 16)
            dve.wait_ge(ends_loaded, 16)

            def expert(e, u, more):
                first, end = bounds(dve, e)
                if more:
                    ahead(e + 1, (u + 1) % UNROLL, first)
                with dve.Fori(first, end) as b:
                    scale_y(b - 1)
                    for n in range(2):
                        cols = slice(n * QUARTER, (n + 1) * QUARTER)
                        dve.wait_ge(silu_done[n], through(b))
                        dve.wait_ge(hid_tr[n], through(b - 1))
                        nc.vector.tensor_tensor(hid[:, cols], p_up[:, cols], gate_s[:, n, :], ALU.mult).then_inc(hid_done[n], 1)
                    for n in range(2):
                        dve.wait_ge(hid_hi_done[n], through(b))
                        nc.vector.tensor_tensor(hid_lo[:, 2 * n:2 * n + 2, :].rearrange("p k n -> p (k n)"), p_hid[n][:, 0:2 * P],
                                                hid_hi[:, 2 * n:2 * n + 2, :].bitcast(F32).rearrange("p k n -> p (k n)"), ALU.subtract).then_inc(hid_lo_done[n], 1)
                    low_x(b + 1)
                if more:
                    behind(e + 1, (u + 1) % UNROLL, end)

            all_experts(dve, expert)
            last = dve.value_load(ends[0:1, E + 1:E + 2], min_val=1, max_val=NBLK - 1)
            scale_y(last - 1)

        @block.tensor
        def _(pe):
            def transpose_x(n):
                for k in range(QT):
                    last = nc.tensor.transpose(p_x[n][:, k * P:(k + 1) * P], x_tok[:, (n * QT + k) * P:(n * QT + k + 1) * P], ident[:])
                last.then_inc(x_tr[n], 1)

            def transpose_hid(n):
                for k in range(2):
                    last = nc.tensor.transpose(p_hid[n][:, k * P:(k + 1) * P], hid[:, (2 * n + k) * P:(2 * n + k + 1) * P], ident[:])
                last.then_inc(hid_tr[n], 1)

            pe.wait_ge(consts, 3)
            pe.wait_ge(gathered, 16)
            transpose_x(0)
            transpose_x(1)
            pe.wait_ge(ends_loaded, 16)

            def expert(e, u, more):
                first, end = bounds(pe, e)
                with pe.Fori(first, end) as b:
                    pe.wait_ge(hid_done[1], through(b - 1))
                    pe.wait_ge(x_lo_done[0], through(b))
                    pe.wait_ge(x_lo_done[1], through(b))
                    for k in range(KT):
                        if k % 2 == 0:
                            pe.wait_ge(hi_made[k // 2], made(e))
                            pe.wait_ge(lo_made[k // 2], made(e))
                        for s, (a, w) in enumerate(((x_hi, w_hi), (x_hi, w_lo), (x_lo, w_hi))):
                            for n, out in enumerate((p_gate, p_up)):
                                last = nc.tensor.matmul(out[:], a[:, k, :], w[:, slot(u, k), n * DE:(n + 1) * DE],
                                                        start=(k == 0 and s == 0), stop=(k == KT - 1 and s == 2))
                    last.then_inc(up_done, 1)
                    pe.wait_ge(gathered, 16 * (b + 2))
                    for n in range(2):
                        transpose_x(n)
                        pe.wait_ge(hid_done[n], through(b))
                        pe.wait_ge(hid_lo_done[n], through(b - 1))
                        transpose_hid(n)
                    pe.wait_ge(y_scaled, scaled(b - 1))
                    for k in range(FT):
                        if k % 2 == 0:
                            pe.wait_ge(hid_lo_done[k // 2], through(b))
                            pe.wait_ge(hi_made[UP_KT + k // 2], made(e))
                            pe.wait_ge(lo_made[UP_KT + k // 2], made(e))
                        for s, (a, w) in enumerate(((hid_hi, w_hi), (hid_hi, w_lo), (hid_lo, w_hi))):
                            for n in range(2):
                                last = nc.tensor.matmul(p_y[:, n * QW:(n + 1) * QW], a[:, k, :], w[:, slot(u, KT + k), n * QW:(n + 1) * QW],
                                                        start=(k == 0 and s == 0), stop=(k == FT - 1 and s == 2))
                    last.then_inc(down_done, 1)

            all_experts(pe, expert)


def combine_phase(nc, y_rows, choice_row, choice_gate, x_scaled, ln2_g, ln2_b, out):
    with ExitStack() as ctx:
        sb, ps, sem = allocators(nc, ctx, "combine")
        pairs = lambda name, shape, dt=F32: [sb(f"{name}{i}", shape, dt) for i in range(2)]
        rows = sb("rows6", [P, NA], I32)
        gates = sb("gates6", [P, NA])
        g_row = sb("g_row6", [P, D])
        b_row = sb("b_row6", [P, D])
        half_neg = sb("half_neg6", [P, 1])
        eps = sb("eps6", [P, 1])
        index = [pairs(f"index6_{c}", [P, 1], I32) for c in range(2)]
        gate = pairs("gate6", [P, 2])
        y = [pairs(f"y6_{c}", [P, D]) for c in range(2)]
        xt = pairs("xt6", [P, D])
        res = pairs("res6", [P, D])
        stats = sb("stats6", [P, 2, 6])
        mean_var = pairs("mean_var6", [P, 2])
        rstd = pairs("rstd6", [P, 1])
        shift = pairs("shift6", [P, 1])
        o = pairs("o6", [P, D])
        shift_m = sb("shift_m6", [P, 1])

        pool_passed, dve_passed = sem("pool_passed"), sem("dve_passed")
        consts, rows_loaded, vec_loaded = (sem(n) for n in "consts6 rows_loaded6 vec_loaded6".split())
        y_gathered = [[sem(f"y_gathered{c}_{i}") for i in range(2)] for c in range(2)]
        x_loaded, out_stored = ([sem(f"{n}{i}") for i in range(2)] for n in ("x_loaded6_", "out_stored6_"))
        names = ("idx_copied gate_copied first_scaled second_added x_added stat_done6 aggr_done6 var_eps6 "
                 "rstd_done6 mean_scaled shift_done normed6 g_done b_done")
        primed = [sem(n) for n in names.split()]
        (idx_copied, gate_copied, first_scaled, second_added, x_added, stat_done, aggr_done, var_eps, rstd_done,
         mean_scaled, shift_done, normed, g_done, b_done) = primed
        x_v, out_v = (a.rearrange("(q t p) d -> q t p d", p=P, t=2) for a in (x_scaled, out))
        block = ctx.enter_context(nc.Block())

        def through(t):
            return t + 1 + PRIME

        def arrived(t, par):
            return 8 * (t - par) + 16

        def all_tiles(eng, tile):
            with eng.Fori(0, NT // 2) as pair:
                for par in range(2):
                    tile(pair * 2 + par, par, pair)

        @block.sync
        def _(sp):
            for s in primed:
                sp.sem_inc(s, PRIME)
            for s in out_stored:
                sp.sem_inc(s, 16)
            sp.dma_start(rows[:], choice_row).then_inc(rows_loaded, 16)
            sp.dma_start(gates[:], choice_gate).then_inc(rows_loaded, 16)
            sp.dma_start(g_row[:], ln2_g.to_broadcast([P, D])).then_inc(vec_loaded, 16)
            sp.dma_start(b_row[:], ln2_b.to_broadcast([P, D])).then_inc(vec_loaded, 16)

            def tile(t, par, pair):
                sp.wait_ge(x_added, through(t - 2))
                sp.dma_start(xt[par][:].rearrange("p (a n) -> p a n", a=1), x_v[bass.ds(pair, 1), par].rearrange("a p n -> p a n")).then_inc(x_loaded[par], 16)

            all_tiles(sp, tile)

        @block.gpsimd
        def _(pool):
            nc.gpsimd.memset(half_neg[:], -0.5).then_inc(consts, 1)
            nc.gpsimd.memset(eps[:], 1e-5).then_inc(consts, 1)
            pool.wait_ge(consts, 2)
            pool.wait_ge(rows_loaded, 32)
            pool.wait_ge(vec_loaded, 32)

            def gather(t, par):
                pool.wait_ge(second_added, through(t - 2))
                for c in range(2):
                    nc.gpsimd.tensor_copy(index[c][par][:], rows[:, bass.ds(t + c * NT, 1)]).then_inc(idx_copied, 1)
                nc.gpsimd.tensor_copy(gate[par][:].rearrange("p (c a) -> p c a", a=1),
                                      gates[:].rearrange("p (c t) -> p c t", c=2)[:, :, bass.ds(t, 1)]).then_inc(gate_copied, 1)
                pool.wait_ge(idx_copied, 2 * t + 2 + PRIME)
                pool.sem_inc(pool_passed, 1)
                for c in range(2):
                    nc.gpsimd.indirect_dma_start(y[c][par][:], None, y_rows,
                                                 bass.IndirectOffsetOnAxis(ap=index[c][par][:].bitcast(U32), axis=0)).then_inc(y_gathered[c][par], 16)

            gather(0, 0)
            gather(1, 1)

            def inverse_std(t, par):
                V = through(t)
                pool.wait_ge(aggr_done, V)
                pool.wait_ge(normed, V - 2)
                nc.gpsimd.tensor_tensor(rstd[par][:], mean_var[par][:, 1:2], eps[:], ALU.add).then_inc(var_eps, 1)
                pool.wait_ge(var_eps, V)
                nc.gpsimd.tensor_tensor(rstd[par][:], rstd[par][:], half_neg[:], ALU.pow).then_inc(rstd_done, 1)

            def add_row(t, par):
                pool.wait_ge(g_done, through(t))
                nc.gpsimd.tensor_tensor(o[par][:], o[par][:], b_row[:], ALU.add).then_inc(b_done, 1)

            inverse_std(0, 0)
            with pool.Fori(0, NT // 2 - 1) as pair:
                for par in range(2):
                    t = pair * 2 + par
                    gather(t + 2, par)
                    inverse_std(t + 1, 1 - par)
                    add_row(t, par)
            inverse_std(NT - 1, 1)
            add_row(NT - 2, 0)
            add_row(NT - 1, 1)

        @block.scalar
        def _(act):
            act.wait_ge(rows_loaded, 32)

            def scale_first(t, par):
                act.wait_ge(y_gathered[0][par], arrived(t, par))
                act.wait_ge(gate_copied, through(t))
                nc.scalar.activation(y[0][par][:], y[0][par][:], ACT.Copy, scale=gate[par][:, 0:1]).then_inc(first_scaled, 1)

            def store(t, par, pair):
                act.wait_ge(b_done, through(t))
                act.dma_start(out_v[bass.ds(pair, 1), par].rearrange("a p n -> p a n"), o[par][:].rearrange("p (a n) -> p a n", a=1)).then_inc(out_stored[par], 16)

            def normalise(t, par):
                V = through(t)
                act.wait_ge(shift_done, V)
                act.wait_ge(out_stored[par], arrived(t, par))
                nc.scalar.activation(o[par][:], res[par][:], ACT.Identity, bias=shift[par][:], scale=rstd[par][:]).then_inc(normed, 1)

            scale_first(0, 0)
            scale_first(1, 1)
            normalise(0, 0)
            with act.Fori(0, NT // 2 - 1) as pair:
                scale_first(pair * 2 + 2, 0)
                normalise(pair * 2 + 1, 1)
                store(pair * 2, 0, pair)
                scale_first(pair * 2 + 3, 1)
                normalise(pair * 2 + 2, 0)
                store(pair * 2 + 1, 1, pair)
            normalise(NT - 1, 1)
            store(NT - 2, 0, NT // 2 - 1)
            store(NT - 1, 1, NT // 2 - 1)
            act.wait_ge(out_stored[0], 8 * NT + 16)
            act.wait_ge(out_stored[1], 8 * NT + 16)

        @block.vector
        def _(dve):
            dve.wait_ge(vec_loaded, 32)

            def scale_rows(t, par):
                V = through(t)
                dve.wait_ge(normed, V)
                nc.vector.tensor_tensor(o[par][:], o[par][:], g_row[:], ALU.mult).then_inc(g_done, 1)

            def tile(t, par, pair):
                V = through(t)
                dve.wait_ge(first_scaled, V)
                dve.wait_ge(gate_copied, V)
                dve.wait_ge(y_gathered[1][par], arrived(t, par))
                dve.wait_ge(normed, V - 2)
                nc.vector.scalar_tensor_tensor(res[par][:], y[1][par][:], gate[par][:, 1:2], y[0][par][:], ALU.mult, ALU.add).then_inc(second_added, 1)
                dve.wait_ge(x_loaded[par], arrived(t, par))
                dve.wait_ge(second_added, V)
                nc.vector.tensor_tensor(res[par][:], res[par][:], xt[par][:], ALU.add).then_inc(x_added, 1)
                dve.wait_ge(x_added, V)
                dve.wait_ge(aggr_done, V - 1)
                for h in range(2):
                    nc.vector.bn_stats(stats[:, h, :], res[par][:, h * QW:(h + 1) * QW]).then_inc(stat_done, 1)
                dve.wait_ge(shift_done, V - 2)
                dve.wait_ge(stat_done, 2 * t + 2 + PRIME)
                dve.sem_inc(dve_passed, 1)
                nc.vector.bn_aggr(mean_var[par][:], stats[:]).then_inc(aggr_done, 1)
                dve.wait_ge(rstd_done, V)
                dve.wait_ge(mean_scaled, V - 1)
                dve.wait_ge(shift_done, V - 1)
                nc.vector.tensor_scalar(shift_m[:], mean_var[par][:, 0:1], rstd[par][:], None, ALU.mult).then_inc(mean_scaled, 1)
                dve.wait_ge(mean_scaled, V)
                nc.vector.tensor_scalar(shift[par][:], shift_m[:], -1.0, None, ALU.mult).then_inc(shift_done, 1)

            tile(0, 0, 0)
            with dve.Fori(0, NT // 2 - 1) as pair:
                tile(pair * 2 + 1, 1, pair)
                scale_rows(pair * 2, 0)
                tile(pair * 2 + 2, 0, pair)
                scale_rows(pair * 2 + 1, 1)
            tile(NT - 1, 1, 0)
            scale_rows(NT - 2, 0)
            scale_rows(NT - 1, 1)


def layer(nc, x, c, ada_w, ada_b, ln1_g, ln1_b, ln2_g, ln2_b, w_in, conv_w, a_log, dt_bias, norm_g, w_out,
          w_grp, b_grp, w_exp, b_exp, w_gate, w_up, w_down, out):
    def scratch(name, shape, dtype=F32):
        return nc.dram_tensor(name, shape, dtype).ap()

    mod_rows = scratch("mod_rows", (1, 6 * D))
    hm_split = scratch("hm_split", (NQ, P, 2, KT, QW))
    gate_scalars = scratch("gate_scalars", (P, ITEMS * NSC * QT))
    mixed = scratch("mixed", (ITEMS, P, QW))
    x_scaled = scratch("x_scaled", (SEQ, D))
    hf = scratch("hf", (SEQ, D))
    logits = scratch("logits", (P, NT * (G + E)))
    slot_token = scratch("slot_token", (P, NBLK), I32)
    choice_row = scratch("choice_row", (P, NA), I32)
    choice_gate = scratch("choice_gate", (P, NA))
    block_ends = scratch("block_ends", (1, E + 2), I32)
    y_rows = scratch("y_rows", (YROWS, D))

    conditioning_phase(nc, c, x, ada_w, ada_b, w_in, a_log, dt_bias, mod_rows, hm_split, gate_scalars)
    deltanet_phase(nc, hm_split, gate_scalars, w_in, conv_w, norm_g, mixed)
    mixer_output_phase(nc, mixed, w_out, x, mod_rows, ln1_g, ln1_b, w_grp, w_exp, x_scaled, hf, logits)
    routing_phase(nc, logits, b_grp, b_exp, slot_token, choice_row, choice_gate, block_ends)
    expert_phase(nc, hf, slot_token, block_ends, mod_rows, w_gate, w_up, w_down, y_rows)
    combine_phase(nc, y_rows, choice_row, choice_gate, x_scaled, ln2_g, ln2_b, out)


def kernel(**inputs):
    import numpy as np
    import concourse.bacc as bacc
    from concourse.bass_utils import run_bass_kernel_spmd

    named = {
        "x": inputs["x"][0], "c": inputs["c"], "ada_w": inputs["ada_w"][0], "ada_b": inputs["ada_b"],
        "ln1_g": inputs["ln1_g"], "ln1_b": inputs["ln1_b"], "ln2_g": inputs["ln2_g"], "ln2_b": inputs["ln2_b"],
        "w_in": inputs["gdn_w_in"][0], "conv_w": inputs["gdn_conv_w"][0], "a_log": inputs["gdn_a_log"],
        "dt_bias": inputs["gdn_dt_bias"], "norm_g": inputs["gdn_norm_g"], "w_out": inputs["gdn_w_out"][0],
        "w_grp": inputs["moe_w_grp"][0], "b_grp": inputs["moe_b_grp"], "w_exp": inputs["moe_w_exp"][0],
        "b_exp": inputs["moe_b_exp"], "w_gate": inputs["moe_w_gate"][0], "w_up": inputs["moe_w_up"][0],
        "w_down": inputs["moe_w_down"][0],
    }
    nc = bacc.Bacc("TRN2", target_bir_lowering=False, num_devices=1)
    arrays, aps = {}, {}
    for name, a in named.items():
        arrays[f"in_{name}"] = np.ascontiguousarray(a)
        aps[name] = nc.dram_tensor(f"in_{name}", a.shape, F32, kind="ExternalInput").ap()
    out = nc.dram_tensor("layer_out", (SEQ, D), F32, kind="ExternalOutput").ap()
    layer(nc, out=out, **aps)
    r = run_bass_kernel_spmd(nc, [arrays], core_ids=[0])
    return r.results[0]["layer_out"].reshape(1, SEQ, D)
```
